# Optimizing a Trainium2 kernel written in Bass

```python
import jax, jax.numpy as jnp
from jax import lax
import numpy as np
import math

D_MODEL = 1024
BATCH = 1
SEQ = 512
DEPTH = 1

CHUNK = 64
CONV_WIDTH = D_MODEL // 2
CONV_GROUPS = 8
CONV_K = 3
ATTN_HEADS = 8
HEAD_DIM = 64
ATTN_WIDTH = ATTN_HEADS * HEAD_DIM
N_BRANCH = 2
Q_BLOCK = 128
FFN_HIDDEN = 2816
FFN_CONV_K = 3
EPS = 1e-6
IN_SPLITS = (CONV_WIDTH, CONV_WIDTH, CONV_WIDTH, ATTN_WIDTH, ATTN_WIDTH, ATTN_WIDTH, ATTN_HEADS, N_BRANCH * D_MODEL)
IN_WIDTH = sum(IN_SPLITS)


def rms_norm(x, g):
    x32 = x.astype(jnp.float32)
    y = x32 * lax.rsqrt(jnp.mean(x32 * x32, axis=-1, keepdims=True) + EPS)
    return y.astype(x.dtype) * g

def causal_dwconv(x, w):
    K = w.shape[0]
    S = x.shape[1]
    xp = jnp.pad(x, ((0, 0), (K - 1, 0), (0, 0)))
    y = xp[:, K - 1:K - 1 + S, :] * w[K - 1]
    for k in range(K - 1):
        y = y + xp[:, k:k + S, :] * w[k]
    return y

def forgetting_attention(q, k, v, log_f):
    B, S, H, hd = q.shape
    scale = 1.0 / np.sqrt(hd).astype(np.float32)
    F = jnp.cumsum(log_f, axis=1).transpose(0, 2, 1)
    qh = q.transpose(0, 2, 1, 3).astype(jnp.float32) * scale
    kh = k.transpose(0, 2, 1, 3).astype(jnp.float32)
    vh = v.transpose(0, 2, 1, 3).astype(jnp.float32)
    nb = S // Q_BLOCK
    q_blocks = qh.reshape(B, H, nb, Q_BLOCK, hd).transpose(2, 0, 1, 3, 4)
    fq_blocks = F.reshape(B, H, nb, Q_BLOCK).transpose(2, 0, 1, 3)
    k_pos = jnp.arange(S)

    def one_block(args):
        q_blk, fq_blk, i = args
        q_pos = i * Q_BLOCK + jnp.arange(Q_BLOCK)
        s = jnp.einsum('bhqd,bhkd->bhqk', q_blk, kh) + fq_blk[..., None] - F[:, :, None, :]
        s = jnp.where(k_pos[None, :] <= q_pos[:, None], s, -jnp.inf)
        p = jax.nn.softmax(s, axis=-1)
        return jnp.einsum('bhqk,bhkd->bhqd', p, vh)

    o = lax.map(one_block, (q_blocks, fq_blocks, jnp.arange(nb)))
    o = o.transpose(1, 0, 3, 2, 4).reshape(B, S, H * hd)
    return o.astype(q.dtype)

def first_inputs(seed: int = 0) -> dict:
    key = jax.random.key(seed)
    ks = jax.random.split(key, 16)
    f32 = jnp.float32
    L = DEPTH
    x = jax.random.normal(ks[0], (BATCH, SEQ, D_MODEL), f32)
    norm_mix_g = 1.0 + 0.02 * jax.random.normal(ks[1], (L, D_MODEL), f32)
    w_in = jax.random.normal(ks[2], (L, D_MODEL, IN_WIDTH), f32) * D_MODEL ** -0.5
    b_f = 2.0 + 0.5 * jax.random.normal(ks[3], (L, ATTN_HEADS), f32)
    b_gate = 0.02 * jax.random.normal(ks[4], (L, N_BRANCH * D_MODEL), f32)
    conv_mix_w = jax.random.normal(ks[5], (L, CONV_K, CONV_WIDTH), f32) * CONV_K ** -0.5
    w_out_conv = jax.random.normal(ks[6], (L, CONV_WIDTH, D_MODEL), f32) * CONV_WIDTH ** -0.5
    w_out_attn = jax.random.normal(ks[7], (L, ATTN_WIDTH, D_MODEL), f32) * ATTN_WIDTH ** -0.5
    w_o = jax.random.normal(ks[8], (L, D_MODEL, D_MODEL), f32) * D_MODEL ** -0.5
    norm_ffn_g = 1.0 + 0.02 * jax.random.normal(ks[9], (L, D_MODEL), f32)
    w_up = jax.random.normal(ks[10], (L, D_MODEL, 2 * FFN_HIDDEN), f32) * D_MODEL ** -0.5
    conv_ffn_w = jax.random.normal(ks[11], (L, FFN_CONV_K, 2 * FFN_HIDDEN), f32) * FFN_CONV_K ** -0.5
    w_down = jax.random.normal(ks[12], (L, FFN_HIDDEN, D_MODEL), f32) * FFN_HIDDEN ** -0.5
    norm_f_g = 1.0 + 0.02 * jax.random.normal(ks[13], (D_MODEL,), f32)
    return {"x": x, "norm_mix_g": norm_mix_g, "w_in": w_in, "b_f": b_f, "b_gate": b_gate,
            "conv_mix_w": conv_mix_w, "w_out_conv": w_out_conv, "w_out_attn": w_out_attn,
            "w_o": w_o, "norm_ffn_g": norm_ffn_g, "w_up": w_up, "conv_ffn_w": conv_ffn_w,
            "w_down": w_down, "norm_f_g": norm_f_g}

def first_block(x, norm_mix_g, w_in, b_f, b_gate, conv_mix_w, w_out_conv, w_out_attn,
              w_o, norm_ffn_g, w_up, conv_ffn_w, w_down, norm_f_g):
    B, S, _ = x.shape
    split_idx = list(np.cumsum(IN_SPLITS)[:-1])
    for l in range(DEPTH):
        h = rms_norm(x, norm_mix_g[l])
        proj = h @ w_in[l]
        cb, cc, cin, q, k, v, f_logit, g_logit = jnp.split(proj, split_idx, axis=-1)
        u = causal_dwconv(cc * cin, conv_mix_w[l])
        y_conv = (cb * u) @ w_out_conv[l]
        log_f = jax.nn.log_sigmoid((f_logit + b_f[l]).astype(jnp.float32))
        o = forgetting_attention(q.reshape(B, S, ATTN_HEADS, HEAD_DIM),
                                 k.reshape(B, S, ATTN_HEADS, HEAD_DIM),
                                 v.reshape(B, S, ATTN_HEADS, HEAD_DIM), log_f)
        y_attn = o @ w_out_attn[l]
        gates = jax.nn.sigmoid(g_logit + b_gate[l])
        g_conv, g_attn = jnp.split(gates, 2, axis=-1)
        x = x + (g_conv * y_conv + g_attn * y_attn) @ w_o[l]
        h = rms_norm(x, norm_ffn_g[l])
        up = causal_dwconv(h @ w_up[l], conv_ffn_w[l])
        a, b = jnp.split(up, 2, axis=-1)
        x = x + (jax.nn.silu(a) * b) @ w_down[l]
    return rms_norm(x, norm_f_g)


DEPTH_2 = 2

N_META = 16
N_MIXERS = 2
EXPAND = 2
D_INNER = EXPAND * D_MODEL
RMS_EPS = 1e-6
N_RWKV_LAYERS = (DEPTH_2 + 1) // 2
N_MLA_LAYERS = DEPTH_2 // 2

RWKV_HEAD = 64
RWKV_HEADS = D_INNER // RWKV_HEAD
DECAY_LORA = 64
AAA_LORA = 64
RWKV_WIDTHS = (D_INNER, D_INNER, D_INNER, D_INNER, DECAY_LORA, AAA_LORA)
N_LERP = len(RWKV_WIDTHS)
RWKV_IN = sum(RWKV_WIDTHS)
GN_EPS = 64e-5

MLA_HEADS = 16
QK_NOPE = 128
QK_ROPE = 64
V_HEAD = 128
Q_LORA = 512
KV_LORA = 256
MLA_IN = Q_LORA + KV_LORA + QK_ROPE + D_INNER
ROPE_THETA = 10000.0


def _rms_norm(x, g):
    xf = x.astype(jnp.float32)
    y = xf * lax.rsqrt(jnp.mean(xf * xf, axis=-1, keepdims=True) + RMS_EPS)
    return (y * g.astype(jnp.float32)).astype(x.dtype)

def _rope(x, pos):
    half = x.shape[-1] // 2
    inv_freq = jnp.exp(-math.log(ROPE_THETA) * jnp.arange(half, dtype=jnp.float32) / half)
    ang = pos[:, None] * inv_freq[None, :]
    ang = ang.reshape((1, ang.shape[0]) + (1,) * (x.ndim - 3) + (half,))
    cos, sin = jnp.cos(ang), jnp.sin(ang)
    xf = x.astype(jnp.float32)
    x1, x2 = xf[..., :half], xf[..., half:]
    return jnp.concatenate([x1 * cos - x2 * sin, x2 * cos + x1 * sin], axis=-1).astype(x.dtype)

def _wkv7_scan(r, decay, k, v, a_vec, b_vec):
    B, L, H, N = r.shape
    xs = tuple(jnp.moveaxis(t.astype(jnp.float32), 1, 0) for t in (r, decay, k, v, a_vec, b_vec))

    def step(S, inp):
        r_t, w_t, k_t, v_t, a_t, b_t = inp
        sa = jnp.einsum('bhij,bhj->bhi', S, a_t)
        S = S * w_t[:, :, None, :] + sa[..., None] * b_t[:, :, None, :] + v_t[..., None] * k_t[:, :, None, :]
        return S, jnp.einsum('bhij,bhj->bhi', S, r_t)

    S0 = jnp.zeros((B, H, N, N), jnp.float32)
    _, ys = lax.scan(step, S0, xs)
    return jnp.moveaxis(ys, 0, 1)

def _rwkv7_mixer(x, mu, w_in, w0, w2, a0, a2, k_k, k_a, r_k, ln_w, ln_b, w_out):
    B, L, _ = x.shape
    H, N = RWKV_HEADS, RWKV_HEAD
    x_prev = jnp.pad(x, ((0, 0), (1, 0), (0, 0)))[:, :-1]
    dx = x_prev - x
    widths = np.array(RWKV_WIDTHS)
    mu_cols = jnp.repeat(mu.T, widths, axis=1, total_repeat_length=RWKV_IN)
    w_comb = jnp.concatenate([w_in, mu_cols * w_in], axis=0)
    h = jnp.concatenate([x, dx], axis=-1) @ w_comb
    r, k, v, g, w_lo, a_lo = jnp.split(h, list(np.cumsum(widths)[:-1]), axis=-1)
    w = -jax.nn.softplus(-(w0 + jnp.tanh(w_lo) @ w2)) - 0.5
    a = jax.nn.sigmoid(a0 + a_lo @ a2)
    heads = lambda t: t.reshape(B, L, H, N)
    r, k, v, w, a = heads(r), heads(k), heads(v), heads(w), heads(a)
    k_k, k_a, r_k = k_k.reshape(H, N), k_a.reshape(H, N), r_k.reshape(H, N)
    kk = (k * k_k).astype(jnp.float32)
    kk = kk / jnp.maximum(jnp.linalg.norm(kk, axis=-1, keepdims=True), 1e-12)
    k = k * (1 + (a - 1) * k_a)
    decay = jnp.exp(-jnp.exp(w.astype(jnp.float32)))
    y = _wkv7_scan(r, decay, k, v, -kk, kk * a.astype(jnp.float32))
    mean = jnp.mean(y, axis=-1, keepdims=True)
    var = jnp.mean(jnp.square(y - mean), axis=-1, keepdims=True)
    y = ((y - mean) * lax.rsqrt(var + GN_EPS)).reshape(B, L, D_INNER)
    y = y * ln_w.astype(jnp.float32) + ln_b.astype(jnp.float32)
    bonus = (jnp.sum(r * k * r_k, axis=-1, keepdims=True) * v).reshape(B, L, D_INNER)
    y = (y + bonus.astype(jnp.float32)).astype(x.dtype) * jax.nn.silu(g)
    return y @ w_out

def _causal_block_attention(q_nope, q_rope, k_nope, k_rope, v):
    L = q_nope.shape[1]
    scale = (QK_NOPE + QK_ROPE) ** -0.5
    neg = jnp.finfo(jnp.float32).min
    bounds = [(0, N_META)] + [(s, min(s + Q_BLOCK, L)) for s in range(N_META, L, Q_BLOCK)]
    outs = []
    for s, e in bounds:
        sc = (jnp.einsum('bqhd,bkhd->bhqk', q_nope[:, s:e], k_nope[:, :e])
              + jnp.einsum('bqhr,bkr->bhqk', q_rope[:, s:e], k_rope[:, :e])).astype(jnp.float32) * scale
        mask = jnp.arange(s, e)[:, None] >= jnp.arange(e)[None, :]
        p = jax.nn.softmax(jnp.where(mask, sc, neg), axis=-1).astype(v.dtype)
        outs.append(jnp.einsum('bhqk,bkhd->bqhd', p, v[:, :e]))
    return jnp.concatenate(outs, axis=1)

def _mla_mixer(x, pos, w_in, q_norm, w_q_up, kv_norm, w_kv_up, w_out):
    B, L, _ = x.shape
    H = MLA_HEADS
    h = x @ w_in
    c_q, c_kv, k_rope, g = jnp.split(h, [Q_LORA, Q_LORA + KV_LORA, Q_LORA + KV_LORA + QK_ROPE], axis=-1)
    q = (_rms_norm(c_q, q_norm) @ w_q_up).reshape(B, L, H, QK_NOPE + QK_ROPE)
    q_nope, q_rope = q[..., :QK_NOPE], _rope(q[..., QK_NOPE:], pos)
    kv = (_rms_norm(c_kv, kv_norm) @ w_kv_up).reshape(B, L, H, QK_NOPE + V_HEAD)
    k_nope, v = kv[..., :QK_NOPE], kv[..., QK_NOPE:]
    k_rope = _rope(k_rope, pos)
    o = _causal_block_attention(q_nope, q_rope, k_nope, k_rope, v).reshape(B, L, D_INNER)
    return (o * jax.nn.silu(g)) @ w_out

def second_inputs(seed: int = 0) -> dict:
    key = jax.random.key(seed)
    ks = jax.random.split(key, 24)
    f32 = jnp.float32
    nrm = lambda k, shape, s: jax.random.normal(k, shape, f32) * s
    NR, NM = N_RWKV_LAYERS, N_MLA_LAYERS
    return {
        "x": nrm(ks[0], (BATCH, SEQ, D_MODEL), 1.0),
        "meta_tokens": nrm(ks[1], (N_META, D_MODEL), 1.0),
        "norm_pre": 1.0 + nrm(ks[2], (DEPTH_2, D_MODEL), 0.02),
        "norm_post": 1.0 + nrm(ks[3], (DEPTH_2, D_MODEL), 0.02),
        "rwkv_mu": jax.random.uniform(ks[4], (NR, N_LERP, D_MODEL), f32),
        "rwkv_w_in": nrm(ks[5], (NR, D_MODEL, RWKV_IN), D_MODEL ** -0.5),
        "rwkv_w0": -2.0 + nrm(ks[6], (NR, D_INNER), 0.5),
        "rwkv_w2": nrm(ks[7], (NR, DECAY_LORA, D_INNER), 0.5 * DECAY_LORA ** -0.5),
        "rwkv_a0": nrm(ks[8], (NR, D_INNER), 0.1),
        "rwkv_a2": nrm(ks[9], (NR, AAA_LORA, D_INNER), 0.5 * AAA_LORA ** -0.5),
        "rwkv_k_k": 0.85 + nrm(ks[10], (NR, D_INNER), 0.05),
        "rwkv_k_a": 1.0 + nrm(ks[11], (NR, D_INNER), 0.05),
        "rwkv_r_k": nrm(ks[12], (NR, D_INNER), 0.1),
        "rwkv_ln_w": 1.0 + nrm(ks[13], (NR, D_INNER), 0.02),
        "rwkv_ln_b": nrm(ks[14], (NR, D_INNER), 0.02),
        "rwkv_w_out": nrm(ks[15], (NR, D_INNER, D_MODEL), D_INNER ** -0.5),
        "mla_w_in": nrm(ks[16], (NM, D_MODEL, MLA_IN), D_MODEL ** -0.5),
        "mla_q_norm": 1.0 + nrm(ks[17], (NM, Q_LORA), 0.02),
        "mla_w_q_up": nrm(ks[18], (NM, Q_LORA, MLA_HEADS * (QK_NOPE + QK_ROPE)), Q_LORA ** -0.5),
        "mla_kv_norm": 1.0 + nrm(ks[19], (NM, KV_LORA), 0.02),
        "mla_w_kv_up": nrm(ks[20], (NM, KV_LORA, MLA_HEADS * (QK_NOPE + V_HEAD)), KV_LORA ** -0.5),
        "mla_w_out": nrm(ks[21], (NM, D_INNER, D_MODEL), D_INNER ** -0.5),
    }

def second_block(x, meta_tokens, norm_pre, norm_post,
              rwkv_mu, rwkv_w_in, rwkv_w0, rwkv_w2, rwkv_a0, rwkv_a2,
              rwkv_k_k, rwkv_k_a, rwkv_r_k, rwkv_ln_w, rwkv_ln_b, rwkv_w_out,
              mla_w_in, mla_q_norm, mla_w_q_up, mla_kv_norm, mla_w_kv_up, mla_w_out):
    B = x.shape[0]
    meta = jnp.broadcast_to(meta_tokens.astype(x.dtype)[None], (B, N_META, D_MODEL))
    h = jnp.concatenate([meta, x], axis=1)
    pos = jnp.arange(h.shape[1], dtype=jnp.float32)
    for i in range(DEPTH_2):
        j = i // N_MIXERS
        u = _rms_norm(h, norm_pre[i])
        if i % N_MIXERS == 0:
            m = _rwkv7_mixer(u, rwkv_mu[j], rwkv_w_in[j], rwkv_w0[j], rwkv_w2[j], rwkv_a0[j], rwkv_a2[j],
                             rwkv_k_k[j], rwkv_k_a[j], rwkv_r_k[j], rwkv_ln_w[j], rwkv_ln_b[j], rwkv_w_out[j])
        else:
            m = _mla_mixer(u, pos, mla_w_in[j], mla_q_norm[j], mla_w_q_up[j], mla_kv_norm[j],
                           mla_w_kv_up[j], mla_w_out[j])
        h = h + _rms_norm(m, norm_post[i])
    return h[:, N_META:]


def setup_inputs(seed=0):
    out = dict(first_inputs(seed))
    for name, value in second_inputs(seed + 1).items():
        if name != "x":
            out[name + "_2"] = value
    return out


def reference(
    x, norm_mix_g, w_in, b_f, b_gate, conv_mix_w, w_out_conv, w_out_attn, w_o, norm_ffn_g, w_up,
    conv_ffn_w, w_down, norm_f_g, meta_tokens_2, norm_pre_2, norm_post_2, rwkv_mu_2,
    rwkv_w_in_2, rwkv_w0_2, rwkv_w2_2, rwkv_a0_2, rwkv_a2_2, rwkv_k_k_2, rwkv_k_a_2, rwkv_r_k_2,
    rwkv_ln_w_2, rwkv_ln_b_2, rwkv_w_out_2, mla_w_in_2, mla_q_norm_2, mla_w_q_up_2,
    mla_kv_norm_2, mla_w_kv_up_2, mla_w_out_2,
):
    x = first_block(
        x, norm_mix_g, w_in, b_f, b_gate, conv_mix_w, w_out_conv, w_out_attn, w_o, norm_ffn_g,
        w_up, conv_ffn_w, w_down, norm_f_g,
    )
    return second_block(
        x, meta_tokens_2, norm_pre_2, norm_post_2, rwkv_mu_2, rwkv_w_in_2, rwkv_w0_2, rwkv_w2_2,
        rwkv_a0_2, rwkv_a2_2, rwkv_k_k_2, rwkv_k_a_2, rwkv_r_k_2, rwkv_ln_w_2, rwkv_ln_b_2,
        rwkv_w_out_2, mla_w_in_2, mla_q_norm_2, mla_w_q_up_2, mla_kv_norm_2, mla_w_kv_up_2,
        mla_w_out_2,
    )


_drawn_inputs = setup_inputs


def setup_inputs(seed=0):
    import zlib

    import numpy as np

    out = dict(_drawn_inputs(seed))
    spreads = {}
    factors = {'b_gate': 5.887,
     'rwkv_k_k_2': 3.159,
     'rwkv_ln_w_2': 3.003,
     'mla_q_norm_2': 5.014,
     'mla_kv_norm_2': 3.589,
     'rwkv_ln_b_2': 3.854}
    for name, (base, spread) in spreads.items():
        noise = np.random.default_rng([zlib.crc32(name.encode()), seed]).standard_normal(out[name].shape)
        drawn = base * np.exp(spread * noise) if base else spread * noise
        out[name] = __import__('jax').numpy.asarray(drawn.astype(out[name].dtype))
    for name, factor in factors.items():
        out[name] = (out[name] * factor).astype(out[name].dtype)
    return out
```

```python
import itertools
import math
from contextlib import ExitStack

import numpy as np

import concourse.bass as bass
from concourse import mybir

F32 = mybir.dt.float32
F32R = mybir.dt.float32r
BF16 = mybir.dt.bfloat16
ALU = mybir.AluOpType
ACT = mybir.ActivationFunctionType
AX_X = mybir.AxisListType.X
AX_XY = mybir.AxisListType.XY

P = 128
D = 1024
KD = D // P
T1 = 512
N_META = 16
T2 = T1 + N_META
QB = T1 // P
HEADS1, HD1 = 8, 64
FFN = 2816
KF = FFN // P
EPS = 1e-6
HALVES1 = [(0, T1)]
HALVES2 = [(0, T2 // 2), (T2 // 2, T2 // 2)]
NEG = -1e30

RH = 32
PAIRS = RH // 2
DI = 2048
C = 64
NC_ = 9
PAD = NC_ * C - T2
TP = NC_ * C
GN_EPS = 64e-5

MH = 16
ROPE = 64
MSCALE = (128 + ROPE) ** -0.5

ROWS = [
    [("cf0", 44), ("cf1", 44), ("w0", 16), ("a0", 16), ("qn", 4), ("kvn", 2)],
    [("cf2", 44), ("mu", 48), ("g_mix", 8), ("g_ffn", 8), ("g_f", 8), ("cm", 12)],
    [("k_k", 16), ("k_a", 16), ("r_k", 16), ("ln_w", 16), ("ln_b", 16), ("b_gate", 16), ("pre", 16), ("post", 16)],
]
COL = {}
for _g, _rows in enumerate(ROWS):
    _at = 0
    for _name, _n in _rows:
        COL[_name] = _g * P + _at
        _at += _n
ROWS_USED = [sum(n for _, n in rows) for rows in ROWS]

UNITS = {}
_u = 0
for _name, _n in [("conv", 12), ("q", 4), ("k", 4), ("f", 1), ("v", 4), ("gate", 16), ("out", 8), ("o", 8),
                  ("up", 44), ("down", 22), ("wkv_out", 16), ("mla_in", 23), ("heads", 16), ("mla_out", 16)]:
    UNITS[_name] = (_u, _n)
    _u += _n


def program(nc, io, out):
    with ExitStack() as base:
        def sb(name, shape, dt=F32, stack=base):
            return stack.enter_context(nc.sbuf_tensor(name, shape, dt))

        PARTS_KB = 20

        def sem(name):
            return base.enter_context(nc.semaphore(name))

        def region(kb):
            at = [int((kb + PARTS_KB) * 1024)]

            def put(name, shape, dt=F32):
                size = 4
                for n in shape[1:]:
                    size *= n
                with ExitStack() as room:
                    if at[0]:
                        room.enter_context(nc.sbuf_tensor(f"below_{name}", [P, at[0] // 4], F32))
                    buf = room.enter_context(nc.sbuf_tensor(name, shape, dt))
                at[0] += -(-size // 64) * 64
                put.end = at[0] / 1024 - PARTS_KB
                return buf
            return put

        ps = base.enter_context(nc.psum_tensor("ps", [P, 8, 512], F32))

        ident = sb("ident", [P, P])
        ones = sb("ones", [P, P])
        causal = sb("causal", [P, P])
        ident_b, causal_b = sb("ident_b", [P, P], BF16), sb("causal_b", [P, P], BF16)
        sel = sb("sel", [HEADS1, HEADS1, P])
        params = sb("params", [P, 3 * P])
        b_f = sb("b_f", [HEADS1, 1])
        eps_col = sb("eps_col", [P, 4])
        raw = [sb(f"raw{s}", [P, 1280]) for s in range(2)]
        wa_in = sb("wa_in", [P, T2])
        omka = sb("omka", [P, PAIRS])
        xT = sb("xT", [P, KD, T2])

        half_in = [sem(f"half_in{s}") for s in range(2)]
        put = region(-PARTS_KB)
        w_hi = [put(f"w_hi{s}", [P, 1280], F32R) for s in range(2)]
        w_lo = [put(f"w_lo{s}", [P, 1280], F32R) for s in range(2)]
        landed = [sem(f"landed{s}") for s in range(2)]
        unit_taken = sem("unit_taken")
        split_hi = sem("split_hi")
        split_ready = sem("split_ready")
        unit_done = sem("unit_done")

        def prm(name, j=0, n=1):
            return params[:, COL[name] + j:COL[name] + j + n]

        def prm_at(name, j):
            return params[:, bass.ds(j + COL[name], 1)]

        def load_unit(sp, u, s, src, first=False):
            if not first:
                sp.wait_ge(split_ready, u - 1)
            _, k, n = src.shape
            sp.dma_start(raw[s][:, 0:k * n].rearrange("p (k n) -> p k n", k=k), src).then_inc(landed[s], 16)

        def landings(u, s):
            return (u - s) * 8 + 16

        def split_unit(pool, u, s, width=1024, first=False):
            pool.wait_ge(landed[s], landings(u, s))
            if not first:
                pool.wait_ge(unit_done, u - 1)
            pool.sem_inc(unit_taken, 1)
            nc.gpsimd.tensor_scalar(w_hi[s][:, 0:width], raw[s][:, 0:width], 1.0, 0.0, ALU.mult,
                                    ALU.add).then_inc(split_hi, 1)
            pool.wait_ge(split_hi, u + 1)
            nc.gpsimd.tensor_tensor(w_lo[s][:, 0:width], raw[s][:, 0:width], w_hi[s][:, 0:width].bitcast(F32),
                                    ALU.subtract).then_inc(split_ready, 1)
            pool.wait_ge(split_ready, u + 1)

        def block_of(s, b, n=P):
            return w_hi[s][:, b * P:b * P + n], w_lo[s][:, b * P:b * P + n]

        def product(dst, w, x, start, stop):
            nc.tensor.matmul(dst, w[0], x[0], start=start, stop=False)
            nc.tensor.matmul(dst, w[0], x[1], start=False, stop=False)
            return nc.tensor.matmul(dst, w[1], x[0], start=False, stop=stop)

        def wcols(w, c0, k=KD, n=P):
            return w.rearrange("(k p) n -> p k n", p=P)[:, 0:k, c0:c0 + n]

        def wcols_at(w, c, n=P):
            return w.rearrange("(k p) n -> p k n", p=P)[:, :, bass.ds(c, n)]

        sq_ready = sem("sq_ready")
        sq_summed = sem("sq_summed")
        ln_ready = sem("ln_ready")
        rs_ready = sem("rs_ready")
        y_ready = sem("y_ready")
        y_hi_ready = sem("y_hi_ready")
        y_lo_ready = sem("y_lo_ready")
        act_hi_ready = sem("act_hi_ready")
        even_lo_ready, odd_lo_ready = sem("even_lo_ready"), sem("odd_lo_ready")
        tiles_before = [0]
        norms_before = [0]

        class Norm:
            def __init__(self, x, tiles, halves, width, gain, bank, kb, slots=2):
                n = norms_before[0]
                put = region(kb)
                self.sq = put(f"norm{n}_sq", [P, 2, T2])
                self.r = put(f"norm{n}_r", [P, T2])
                self.ln = put(f"norm{n}_ln", [P, T2])
                self.y = put(f"norm{n}_y", [P, slots, T2])
                self.x, self.tiles, self.halves, self.gain, self.bank = x, tiles, halves, gain, bank
                self.cols = halves[-1][0] + halves[-1][1]
                self.width = width
                self.t0, self.n0 = tiles_before[0], norms_before[0]
                tiles_before[0] += tiles
                norms_before[0] += 1

            def act(self, act, wait_x):
                for j in range(self.tiles):
                    wait_x(act, j)
                    if self.t0 + j >= 2:
                        act.wait_ge(sq_summed, self.t0 + j - 1)
                    nc.scalar.activation(self.sq[:, j % 2, 0:self.cols], self.x(j), ACT.Square).then_inc(sq_ready, 1)
                act.wait_ge(sq_summed, self.t0 + self.tiles)
                src = ps[:, self.bank, 0:self.cols] if len(self.halves) == 1 else \
                    ps[:, self.bank:self.bank + 2, 0:self.halves[0][1]]
                dst = self.ln[:, 0:self.cols] if len(self.halves) == 1 else \
                    self.ln[:, 0:self.cols].rearrange("p (a b) -> p a b", a=2)
                nc.scalar.activation(dst, src, ACT.Ln, scale=1.0 / self.width, bias=eps_col[:, 0:1]).then_inc(ln_ready, 1)
                act.wait_ge(ln_ready, self.n0 + 1)
                nc.scalar.activation(self.r[:, 0:self.cols], self.ln[:, 0:self.cols], ACT.Exp,
                                     scale=-0.5).then_inc(rs_ready, 1)

            def pe(self, pe):
                for j in range(self.tiles):
                    pe.wait_ge(sq_ready, self.t0 + j + 1)
                    for h, (at, n) in enumerate(self.halves):
                        mm = nc.tensor.matmul(ps[:, self.bank + h, 0:n], ones[:], self.sq[:, j % 2, at:at + n],
                                              start=(j == 0), stop=(j == self.tiles - 1))
                    mm.then_inc(sq_summed, 1)

            def dve(self, dve, hi=None, lo=None, y=None):
                dve.wait_ge(rs_ready, self.n0 + 1)
                for j in range(self.tiles):
                    n = self.t0 + j
                    dst = y(j) if y else self.y[:, j % 2, 0:self.cols]
                    nc.vector.scalar_tensor_tensor(out=dst, in0=self.x(j), scalar=self.gain(j),
                                                   in1=self.r[:, 0:self.cols], op0=ALU.mult,
                                                   op1=ALU.mult).then_inc(y_ready, 1)
                    dve.wait_ge(y_ready, n + 1)
                    if hi:
                        nc.vector.tensor_copy(hi(j), dst).then_inc(y_hi_ready, 1)
                        hi_before[0] += 1
                        dve.wait_ge(y_hi_ready, hi_before[0])
                        nc.vector.tensor_tensor(lo(j), dst, hi(j).bitcast(F32), ALU.subtract).then_inc(y_lo_ready, 1)
                if hi:
                    dve.wait_ge(y_lo_ready, hi_before[0])
            def dve_parts(self, dve, hi, lo):
                dve.wait_ge(rs_ready, self.n0 + 1)
                self.p0 = parted_before[0]
                parted_before[0] += self.tiles
                for j in range(self.tiles):
                    if j >= 4 and j % 2:
                        dve.wait_ge(odd_lo_ready, (self.p0 + j - 4) // 2 + 1)
                    nc.vector.scalar_tensor_tensor(out=self.y[:, j % 4, 0:self.cols], in0=self.x(j), scalar=self.gain(j),
                                                   in1=self.r[:, 0:self.cols], op0=ALU.mult, op1=ALU.mult).then_inc(y_ready, 1)
                    if j % 2:
                        dve.wait_ge(y_ready, self.t0 + j)
                        dve.wait_ge(act_hi_ready, self.p0 + j)
                        nc.vector.tensor_tensor(lo(j - 1), self.y[:, (j - 1) % 4, 0:self.cols], hi(j - 1).bitcast(F32),
                                                ALU.subtract).then_inc(even_lo_ready, 1)
                dve.wait_ge(even_lo_ready, (self.p0 + self.tiles) // 2)

            def act_parts(self, act, hi, p0):
                for j in range(self.tiles):
                    act.wait_ge(y_ready, self.t0 + j + 1)
                    nc.scalar.activation(hi(j), self.y[:, j % 4, 0:self.cols], ACT.Copy).then_inc(act_hi_ready, 1)

            def pool_parts(self, pool, hi, lo, p0):
                for j in range(1, self.tiles, 2):
                    pool.wait_ge(act_hi_ready, p0 + j + 1)
                    pool.wait_ge(y_ready, self.t0 + j + 1)
                    nc.gpsimd.tensor_tensor(lo(j), self.y[:, j % 4, 0:self.cols], hi(j).bitcast(F32),
                                            ALU.subtract).then_inc(odd_lo_ready, 1)
                    pool.wait_ge(odd_lo_ready, (p0 + j + 1) // 2)
        hi_before = [0]
        parted_before = [0]

        s_x = sem("s_x")
        s_in = sem("s_in")
        cst = sem("cst")
        zeroed = sem("zeroed")
        p_turned = sem("p_turned")
        p_copied = sem("p_copied")
        x_turned = sem("x_turned")
        x_copied = sem("x_copied")

        low = region(0)
        gates = low("gates", [P, 16, T1])
        conv_hi = low("conv_hi", [P, 4, T1], F32R)
        conv_lo = low("conv_lo", [P, 4, T1], F32R)
        o_rows = low("o_rows", [P, QB, 512])
        negF = low("negF", [HEADS1, T1])
        h_hi = low("h_hi", [P, KD, T1], F32R)
        h_lo = low("h_lo", [P, KD, T1], F32R)
        qT = low("qT", [P, 4, T1])
        kT = low("kT", [P, 4, T1])
        v_rows = low("v_rows", [P, QB, 512])
        put = region(0)
        x_rows = put("x_rows", [P, QB, D])
        p_rows = put("p_rows", [P, 3, P])
        h_parts = (lambda j: h_hi[:, j, :]), (lambda j: h_lo[:, j, :])
        x_kept = nc.dram_tensor("x_kept", [P, KD, T1], F32, kind="Internal").ap()

        w_in = io["w_in"][0]
        CB, CC, CIN, QC, KC, VC, FC_, GC = 0, 512, 1024, 1536, 2048, 2560, 3072, 3080

        def conv_src(j):
            m, part = j // 3, j % 3
            return wcols(w_in, [CC, CIN, CB][part] + P * m)

        norm_mix = Norm(lambda j: xT[:, j, 0:T1], KD, HALVES1, D, lambda j: prm("g_mix", j), 6, 130, slots=4)

        with nc.Block() as block:
            @block.sync
            def _(sp):
                sp.dma_start(x_rows[:], io["x"][0].rearrange("(t p) d -> p t d", p=P)).then_inc(s_in, 16)
                v2 = {
                    "cf0": io["conv_ffn_w"][0, 0].rearrange("(r c) -> r c", c=P),
                    "cf1": io["conv_ffn_w"][0, 1].rearrange("(r c) -> r c", c=P),
                    "cf2": io["conv_ffn_w"][0, 2].rearrange("(r c) -> r c", c=P),
                    "cm": io["conv_mix_w"][0].rearrange("k (r c) -> (k r) c", c=P),
                    "mu": io["rwkv_mu_2"][0].rearrange("k (r c) -> (k r) c", c=P),
                    "pre": io["norm_pre_2"].rearrange("k (r c) -> (k r) c", c=P),
                    "post": io["norm_post_2"].rearrange("k (r c) -> (k r) c", c=P),
                    "g_f": io["norm_f_g"].rearrange("(r c) -> r c", c=P),
                }
                for name, arg in [("w0", "rwkv_w0_2"), ("a0", "rwkv_a0_2"), ("qn", "mla_q_norm_2"),
                                  ("kvn", "mla_kv_norm_2"), ("g_mix", "norm_mix_g"), ("g_ffn", "norm_ffn_g"),
                                  ("k_k", "rwkv_k_k_2"), ("k_a", "rwkv_k_a_2"), ("r_k", "rwkv_r_k_2"),
                                  ("ln_w", "rwkv_ln_w_2"), ("ln_b", "rwkv_ln_b_2"), ("b_gate", "b_gate")]:
                    v2[name] = io[arg][0].rearrange("(r c) -> r c", c=P)
                for g, rows in enumerate(ROWS):
                    at = 0
                    for name, n in rows:
                        sp.dma_start(p_rows[at:at + n, g, :], v2[name]).then_inc(s_in, 16)
                        at += n
                sp.dma_start(b_f[:], io["b_f"].rearrange("a h -> h a")).then_inc(s_in, 16)
                for u in range(2):
                    load_unit(sp, u, u % 2, conv_src(u), first=True)
                sp.wait_ge(x_copied, KD)
                sp.dma_start(x_kept, xT[:, :, 0:T1]).then_inc(s_x, 16)
                sp.wait_ge(s_x, 16)

            n_in = 16 * (2 + sum(len(r) for r in ROWS))

            @block.gpsimd
            def _(pool):
                nc.gpsimd.memset(ident[:], 0.0).then_inc(zeroed, 1)
                nc.gpsimd.memset(ones[:], 1.0).then_inc(zeroed, 1)
                nc.gpsimd.memset(causal[:], 0.0).then_inc(zeroed, 1)
                nc.gpsimd.memset(sel[:], 0.0).then_inc(zeroed, 1)
                nc.gpsimd.memset(eps_col[:, 0:1], EPS).then_inc(zeroed, 1)
                nc.gpsimd.memset(eps_col[:, 1:2], GN_EPS).then_inc(zeroed, 1)
                nc.gpsimd.memset(eps_col[:, 2:3], 1.0).then_inc(zeroed, 1)
                pool.wait_ge(zeroed, 7)
                nc.gpsimd.affine_select(out=ident[:], in_=ident[:], compare_op=ALU.not_equal, fill=1.0, base=0,
                                        pattern=[[-1, P]], channel_multiplier=1).then_inc(cst, 1)
                pool.wait_ge(cst, 1)
                nc.gpsimd.affine_select(out=causal[:], in_=causal[:], compare_op=ALU.is_ge, fill=NEG, base=0,
                                        pattern=[[-1, P]], channel_multiplier=1).then_inc(cst, 1)
                pool.wait_ge(cst, 2)
                nc.gpsimd.affine_select(out=sel[:], in_=sel[:], compare_op=ALU.not_equal, fill=1.0, base=0,
                                        pattern=[[-1, HEADS1], [0, P]], channel_multiplier=1).then_inc(cst, 1)
                pool.wait_ge(cst, 3)
                for u in range(2):
                    split_unit(pool, u, u % 2, first=True)
                norm_mix.pool_parts(pool, *h_parts, 0)

            @block.tensor
            def _(pe):
                pe.wait_ge(s_in, n_in)
                pe.wait_ge(cst, 1)
                for g in range(3):
                    n = ROWS_USED[g]
                    nc.tensor.transpose(ps[:, 0, g * P:g * P + n], p_rows[0:n, g, :], ident[0:n, 0:n]).then_inc(p_turned, 1)
                for j in range(KD):
                    if j >= 4:
                        pe.wait_ge(x_copied, j - 3)
                    for t in range(QB):
                        mm = nc.tensor.transpose(ps[:, 1 + j % 4, t * P:t * P + P], x_rows[:, t, j * P:j * P + P], ident[:])
                    mm.then_inc(x_turned, 1)
                norm_mix.pe(pe)

            @block.scalar
            def _(act):
                act.wait_ge(cst, 3)
                nc.scalar.activation(ident_b[:], ident[:], ACT.Copy)
                nc.scalar.activation(causal_b[:], causal[:], ACT.Copy)
                norm_mix.act(act, lambda e, j: e.wait_ge(x_copied, j + 1))
                norm_mix.act_parts(act, h_parts[0], 0)

            @block.vector
            def _(dve):
                dve.wait_ge(p_turned, 3)
                for g in range(3):
                    n = ROWS_USED[g]
                    nc.vector.tensor_copy(params[:, g * P:g * P + n], ps[:, 0, g * P:g * P + n]).then_inc(p_copied, 1)
                for j in range(KD):
                    dve.wait_ge(x_turned, j + 1)
                    nc.vector.tensor_copy(xT[:, j, 0:T1], ps[:, 1 + j % 4, :]).then_inc(x_copied, 1)
                dve.wait_ge(p_copied, 3)
                dve.wait_ge(x_copied, KD)
                norm_mix.dve_parts(dve, *h_parts)

        put = region(129)
        cc = put("cc", [P, 2, T1])
        cin = put("cin", [P, 2, T1])
        cb = put("cb", [P, 2, T1])
        cprod = put("cprod", [P, T1 + 2])
        cu = put("cu", [P, 3, T1])
        cz = put("cz", [P, T1])
        fl = xT[0:HEADS1, 0:6, 0:T1]
        fones = xT[0:HEADS1, 6, 0:T1]
        evac = sem("evac")
        c_step = sem("c_step")
        f_step = sem("f_step")
        f_dve = sem("f_dve")
        v_out = sem("v_out")
        cpad = sem("cpad")
        U_CONV, U_Q, U_F, U_V = (UNITS[n][0] for n in ("conv", "q", "f", "v"))
        U_GATE = UNITS["gate"][0]

        def x_parts(hi, lo):
            return lambda k: (hi[:, k, 0:T1], lo[:, k, 0:T1])

        h_x = x_parts(h_hi, h_lo)

        def strip(pe, u, s, bank, x, first=False, e=None):
            pe.wait_ge(split_ready, u + 1)
            if not first:
                pe.wait_ge(evac, e if e is not None else u - 1)
            for k in range(KD):
                mm = product(ps[:, bank, :], block_of(s, k), x(k), k == 0, k == KD - 1)
            mm.then_inc(unit_done, 1)

        v_src = lambda j: w_in.rearrange("(k p) n -> p k n", p=P)[:, 2 * j:2 * j + 2, VC:VC + 512]

        with nc.Block() as block:
            @block.sync
            def _(sp):
                for j in range(2, 12):
                    load_unit(sp, U_CONV + j, j % 2, conv_src(j))
                with sp.Fori(0, 4) as i:
                    for s in range(2):
                        load_unit(sp, 2 * i + (U_Q + s), s, wcols_at(w_in, 256 * i + (QC + P * s)))
                load_unit(sp, U_F, U_F % 2, wcols(w_in, FC_))
                for j in range(4):
                    load_unit(sp, U_V + j, (U_V + j) % 2, v_src(j))
                for j in range(2):
                    load_unit(sp, U_GATE + j, (U_GATE + j) % 2, wcols(w_in, GC + P * j))

            @block.gpsimd
            def _(pool):
                with pool.Fori(1, (U_F - 1) // 2 + 1) as i:
                    for s in range(2):
                        split_unit(pool, 2 * i + s, s)
                for u in range(U_F - (U_F % 2), U_GATE + 2):
                    split_unit(pool, u, u % 2)

            @block.tensor
            def _(pe):
                for u in range(2):
                    strip(pe, u, u % 2, u % 2, h_x, first=True)
                with pe.Fori(1, U_F // 2) as i:
                    for s in range(2):
                        strip(pe, 2 * i + s, s, s, h_x)
                strip(pe, U_F, U_F % 2, U_F % 2, h_x)
                for j in range(4):
                    u = U_V + j
                    pe.wait_ge(split_ready, u + 1)
                    for k in range(2):
                        for t in range(QB):
                            x = (h_hi[:, 2 * j + k, t * P:t * P + P], h_lo[:, 2 * j + k, t * P:t * P + P])
                            w = (w_hi[u % 2][:, k * 512:k * 512 + 512], w_lo[u % 2][:, k * 512:k * 512 + 512])
                            mm = product(ps[:, 2 + t, :], x, w, j == 0 and k == 0, j == 3 and k == 1)
                    mm.then_inc(unit_done, 1)

            @block.scalar
            def _(act):
                for m in range(4):
                    for part, dst in enumerate((cc, cin, cb)):
                        u = U_CONV + 3 * m + part
                        act.wait_ge(unit_done, u + 1)
                        if m >= 2:
                            act.wait_ge(c_step, 7 * (m - 1))
                        nc.scalar.activation(dst[:, m % 2, :], ps[:, u % 2, :], ACT.Copy).then_inc(evac, 1)
                for j in range(8):
                    u = U_Q + j
                    act.wait_ge(unit_done, u + 1)
                    dst = (qT, kT)[j // 4]
                    nc.scalar.activation(dst[:, j % 4, :], ps[:, u % 2, :], ACT.Copy,
                                         scale=(HD1 ** -0.5, 1.0)[j // 4]).then_inc(evac, 1)
                act.wait_ge(unit_done, U_F + 1)
                nc.scalar.activation(fl[:, 0, :], ps[0:HEADS1, U_F % 2, :], ACT.Identity, bias=b_f[:, 0:1]).then_inc(evac, 1)
                act.wait_ge(evac, U_F + 1)
                nc.scalar.activation(fl[:, 1, :], fl[:, 0, :], ACT.Abs).then_inc(f_step, 1)
                act.wait_ge(f_step, 1)
                nc.scalar.activation(fl[:, 2, :], fl[:, 1, :], ACT.Exp, scale=-1.0).then_inc(f_step, 1)
                act.wait_ge(f_step, 2)
                nc.scalar.activation(fl[:, 3, :], fl[:, 2, :], ACT.Ln, bias=eps_col[0:HEADS1, 2:3]).then_inc(f_step, 1)
                act.wait_ge(unit_done, U_GATE)
                nc.scalar.activation(v_rows[:], ps[:, 2:6, :], ACT.Copy).then_inc(v_out, 1)

            @block.vector
            def _(dve):
                nc.vector.memset(cprod[:, 0:2], 0.0).then_inc(cpad, 1)
                nc.vector.memset(fones, 1.0).then_inc(cpad, 1)
                dve.wait_ge(cpad, 2)
                for m in range(4):
                    s, n = m % 2, 7 * m
                    dve.wait_ge(evac, U_CONV + 3 * m + 3)
                    nc.vector.tensor_tensor(cprod[:, 2:2 + T1], cc[:, s, :], cin[:, s, :], ALU.mult).then_inc(c_step, 1)
                    dve.wait_ge(c_step, n + 1)
                    nc.vector.tensor_scalar(cu[:, 0, :], cprod[:, 2:2 + T1], prm("cm", 8 + m), None, ALU.mult).then_inc(c_step, 1)
                    for k in range(2):
                        dve.wait_ge(c_step, n + 2 + k)
                        nc.vector.scalar_tensor_tensor(out=cu[:, 1 + k, :], in0=cprod[:, k:k + T1], scalar=prm("cm", 4 * k + m),
                                                       in1=cu[:, k, :], op0=ALU.mult, op1=ALU.add).then_inc(c_step, 1)
                    dve.wait_ge(c_step, n + 4)
                    nc.vector.tensor_tensor(cz[:], cu[:, 2, :], cb[:, s, :], ALU.mult).then_inc(c_step, 1)
                    dve.wait_ge(c_step, n + 5)
                    nc.vector.tensor_copy(conv_hi[:, m, :], cz[:]).then_inc(c_step, 1)
                    dve.wait_ge(c_step, n + 6)
                    nc.vector.tensor_tensor(conv_lo[:, m, :], cz[:], conv_hi[:, m, :].bitcast(F32), ALU.subtract).then_inc(c_step, 1)
                    dve.wait_ge(c_step, n + 7)
                dve.wait_ge(evac, U_F + 1)
                dve.wait_ge(f_step, 3)
                nc.vector.tensor_scalar(fl[:, 4, :], fl[:, 0, :], 0.0, None, ALU.min).then_inc(f_dve, 1)
                dve.wait_ge(f_dve, 1)
                nc.vector.tensor_tensor(fl[:, 5, :], fl[:, 3, :], fl[:, 4, :], ALU.subtract).then_inc(f_dve, 1)
                dve.wait_ge(f_dve, 2)
                nc.vector.tensor_tensor_scan(negF[:], fones, fl[:, 5, :], 0.0, ALU.mult, ALU.add).then_inc(f_dve, 1)

        put = region(130)
        bias_k = put("bias_k", [P, HEADS1, T1])
        a_s, a_p, a_pT = (xT[:, 2 * n:2 * n + 2, 0:T1] for n in range(3))
        q_st, k_st = (xT[:, n, 0:T1] for n in (6, 7))
        a_nm = put("a_nm", [P, 2])
        a_sum = put("a_sum", [P, 2])
        a_rs = put("a_rs", [P, 2])
        bias_ps = sem("bias_ps")
        bias_done = sem("bias_done")
        staged = sem("staged")
        a_scores = sem("a_scores")
        a_biased = sem("a_biased")
        a_max = sem("a_max")
        a_exp = sem("a_exp")
        a_turned = sem("a_turned")
        a_pt = sem("a_pt")
        a_rec = sem("a_rec")
        a_pv = sem("a_pv")
        a_out = sem("a_out")
        gate_done = sem("gate_done")
        oT_turned = sem("oT_turned")
        STEPS = 2 * QB

        w_conv, w_attn = io["w_out_conv"][0], io["w_out_attn"][0]
        U_OUT, U_O = UNITS["out"][0], UNITS["o"][0]

        def load_out(sp, m):
            u = U_OUT + m
            s = u % 2
            sp.wait_ge(split_ready, u - 1)
            dst = raw[s][:, 0:1024].rearrange("p (k n) -> p k n", k=KD)
            sp.dma_start(dst[:, 0:4, :], wcols(w_conv, P * m, 4)).then_inc(half_in[s], 16)
            sp.dma_start(dst[:, 4:8, :], wcols(w_attn, P * m, 4)).then_inc(landed[s], 16)

        def split_out(pool, m):
            pool.wait_ge(half_in[(U_OUT + m) % 2], 16 * (m // 2 + 1))
            split_unit(pool, U_OUT + m, (U_OUT + m) % 2)

        with nc.Block() as block:

            @block.sync
            def _(sp):
                with sp.Fori(0, 7) as i:
                    for e in range(2):
                        j = 2 + e
                        load_unit(sp, 2 * i + (U_GATE + j), (U_GATE + j) % 2, wcols_at(w_in, 256 * i + (GC + P * j)))
                for m in range(2):
                    load_out(sp, m)

            @block.gpsimd
            def _(pool):
                with pool.Fori(0, 7) as i:
                    for e in range(2):
                        u = U_GATE + 2 + e
                        split_unit(pool, 2 * i + u, u % 2)
                for m in range(2):
                    split_out(pool, m)

            def half_gate(pe, i, j, half):
                u = U_GATE + j
                if half == 0:
                    pe.wait_ge(split_ready, 4 * i + (u + 1))
                    if j >= 2:
                        pe.wait_ge(gate_done, 4 * i + (j - 1))
                for k in range(4 * half, 4 * half + 4):
                    mm = product(ps[:, u % 2, :], block_of(u % 2, k), h_x(k), k == 0, k == KD - 1)
                if half:
                    mm.then_inc(unit_done, 1)

            @block.tensor
            def _(pe):
                for h in range(HEADS1):
                    if h >= 4:
                        pe.wait_ge(bias_done, h - 3)
                    nc.tensor.matmul(ps[:, 2 + h % 4, :], sel[:, h, :], negF[:], start=True, stop=True).then_inc(bias_ps, 1)

                def scores(i, x):
                    h, b = x // QB, x % QB
                    n, r = (b + 1) * P, slice(h * HD1, h * HD1 + HD1)
                    if x == 0:
                        pe.wait_ge(staged, 2 * i + 2)
                    if x >= 2:
                        pe.wait_ge(a_biased, STEPS * i + (x - 1))
                    bank = 2 + x % 2
                    nc.tensor.matmul(ps[:, bank, 0:n], q_st[r, b * P:b * P + P], k_st[r, 0:n], start=True, stop=False)
                    nc.tensor.matmul(ps[:, bank, b * P:n], ident_b[:], causal_b[:], start=False, stop=True).then_inc(a_scores, 1)

                def turn(i, x):
                    b = x % QB
                    pe.wait_ge(a_exp, STEPS * i + (x + 1))
                    if x >= 2:
                        pe.wait_ge(a_pt, STEPS * i + (x - 1))
                    for c in range(b + 1):
                        mm = nc.tensor.transpose(ps[:, 4 + x % 2, c * P:c * P + P], a_p[:, x % 2, c * P:c * P + P], ident[:])
                    mm.then_inc(a_turned, 1)

                def values(i, x):
                    h, b = x // QB, x % QB
                    pe.wait_ge(a_pt, STEPS * i + (x + 1))
                    if x >= 2:
                        pe.wait_ge(a_out, STEPS * i + (x - 1))
                    for c in range(b + 1):
                        mm = nc.tensor.matmul(ps[:, 6 + x % 2, 0:HD1], a_pT[:, x % 2, c * P:c * P + P],
                                              v_rows[:, c, bass.ds(P * i + HD1 * h, HD1)], start=(c == 0), stop=(c == b))
                    mm.then_inc(a_pv, 1)

                pe.wait_ge(bias_done, HEADS1)
                with pe.Fori(0, 4) as i:
                    if True:
                        pe.wait_ge(gate_done, 4 * i)
                        pe.wait_ge(a_out, STEPS * i)
                    for x in range(STEPS):
                        scores(i, x)
                        if x:
                            values(i, x - 1)
                        half_gate(pe, i, x // 2, x % 2)
                        turn(i, x)
                    values(i, STEPS - 1)

            @block.scalar
            def _(act):
                for h in range(HEADS1):
                    act.wait_ge(bias_ps, h + 1)
                    nc.scalar.activation(bias_k[:, h, :], ps[:, 2 + h % 4, :], ACT.Copy).then_inc(bias_done, 1)
                with act.Fori(0, 4) as i:
                    act.wait_ge(a_scores, STEPS * i)
                    nc.scalar.activation(q_st, qT[:, i, :], ACT.Copy).then_inc(staged, 1)
                    nc.scalar.activation(k_st, kT[:, i, :], ACT.Copy).then_inc(staged, 1)
                    for x in range(STEPS):
                        n = (x % QB + 1) * P
                        act.wait_ge(a_max, STEPS * i + (x + 1))
                        if x >= 2:
                            act.wait_ge(a_turned, STEPS * i + (x - 1))
                            act.wait_ge(a_rec, STEPS * i + (x - 1))
                        else:
                            act.wait_ge(a_turned, STEPS * i)
                            act.wait_ge(a_rec, STEPS * i)
                        nc.scalar.activation(a_p[:, x % 2, 0:n], a_s[:, x % 2, 0:n], ACT.Exp, bias=a_nm[:, x % 2:x % 2 + 1],
                                             accum_out=a_sum[:, x % 2:x % 2 + 1]).then_inc(a_exp, 1)
                        if x % 2:
                            j = x // 2
                            u = U_GATE + j
                            act.wait_ge(unit_done, 4 * i + (u + 1))
                            nc.scalar.activation(gates[:, bass.ds(4 * i + j, 1), :], ps[:, u % 2:u % 2 + 1, :], ACT.Identity,
                                                 bias=prm_at("b_gate", 4 * i + j)).then_inc(gate_done, 1)

            @block.vector
            def _(dve):
                dve.wait_ge(bias_done, HEADS1)

                def finish(i, x):
                    h, b = x // QB, x % QB
                    dve.wait_ge(a_pv, STEPS * i + (x + 1))
                    nc.vector.tensor_scalar(o_rows[:, b, bass.ds(P * i + HD1 * h, HD1)], ps[:, 6 + x % 2, 0:HD1],
                                            a_rs[:, x % 2:x % 2 + 1], None, ALU.mult).then_inc(a_out, 1)
                with dve.Fori(0, 4) as i:
                    for x in range(STEPS):
                        h, n = x // QB, (x % QB + 1) * P
                        dve.wait_ge(a_scores, STEPS * i + (x + 1))
                        if x >= 2:
                            dve.wait_ge(a_exp, STEPS * i + (x - 1))
                        else:
                            dve.wait_ge(a_exp, STEPS * i)
                        nc.vector.tensor_tensor(a_s[:, x % 2, 0:n], ps[:, 2 + x % 2, 0:n],
                                                bias_k[:, 2 * i + h, 0:n], ALU.add).then_inc(a_biased, 1)
                        dve.wait_ge(a_biased, STEPS * i + (x + 1))
                        nc.vector.tensor_reduce(a_nm[:, x % 2:x % 2 + 1], a_s[:, x % 2, 0:n], AX_X, ALU.max,
                                                negate=True).then_inc(a_max, 1)
                        if x:
                            finish(i, x - 1)
                        dve.wait_ge(a_exp, STEPS * i + (x + 1))
                        if x >= 2:
                            dve.wait_ge(a_out, STEPS * i + (x - 1))
                        else:
                            dve.wait_ge(a_out, STEPS * i)
                        nc.vector.reciprocal(a_rs[:, x % 2:x % 2 + 1], a_sum[:, x % 2:x % 2 + 1]).then_inc(a_rec, 1)
                        dve.wait_ge(a_turned, STEPS * i + (x + 1))
                        if x >= 2:
                            dve.wait_ge(a_pv, STEPS * i + (x - 1))
                        else:
                            dve.wait_ge(a_pv, STEPS * i)
                        nc.vector.tensor_copy(a_pT[:, x % 2, 0:n], ps[:, 4 + x % 2, 0:n]).then_inc(a_pt, 1)
                        dve.wait_ge(a_rec, STEPS * i + (x + 1))
                    finish(i, STEPS - 1)

        put = region(58)
        at_hi = put("at_hi", [P, 4, T1], F32R)
        at_lo = put("at_lo", [P, 4, T1], F32R)
        mix_hi = put("mix_hi", [P, KD, T1], F32R)
        mix_lo = put("mix_lo", [P, KD, T1], F32R)
        y_both = put("y_both", [P, 2, 2, T1])
        m_t = put("m_t", [P, 3, T1])
        sig = sem("sig")
        at_h = sem("at_h")
        at_l = sem("at_l")
        branch = sem("branch")
        m_step = sem("m_step")
        U_UP, U_DOWN = UNITS["up"][0], UNITS["down"][0]
        w_o = io["w_o"][0]

        with nc.Block() as block:
            @block.sync
            def _(sp):
                sp.dma_start(xT[:, :, 0:T1], x_kept).then_inc(s_x, 16)
                for m in range(2, 8):
                    load_out(sp, m)
                for m in range(2):
                    load_unit(sp, U_O + m, (U_O + m) % 2, wcols(w_o, P * m))

            @block.gpsimd
            def _(pool):
                for m in range(2, 8):
                    split_out(pool, m)
                for m in range(2):
                    split_unit(pool, U_O + m, (U_O + m) % 2)

            @block.tensor
            def _(pe):
                for j in range(4):
                    for b in range(QB):
                        mm = nc.tensor.transpose(ps[:, 4 + j, b * P:b * P + P], o_rows[:, b, j * P:j * P + P], ident[:])
                    mm.then_inc(oT_turned, 1)
                for m in range(8):
                    u = U_OUT + m
                    s = u % 2
                    pe.wait_ge(split_ready, u + 1)
                    if m >= 2:
                        pe.wait_ge(branch, m - 1)
                    for k in range(4):
                        product(ps[:, 2 * s, :], block_of(s, k), (conv_hi[:, k, :], conv_lo[:, k, :]), k == 0, k == 3)
                    if m == 0:
                        pe.wait_ge(at_l, 4)
                    for k in range(4):
                        mm = product(ps[:, 2 * s + 1, :], block_of(s, 4 + k), (at_hi[:, k, :], at_lo[:, k, :]), k == 0, k == 3)
                    mm.then_inc(unit_done, 1)

            @block.scalar
            def _(act):
                for j in range(4):
                    act.wait_ge(oT_turned, j + 1)
                    nc.scalar.activation(at_hi[:, j, :], ps[:, 4 + j, :], ACT.Copy).then_inc(at_h, 1)
                for j in range(4):
                    nc.scalar.activation(gates[:, 4 * j:4 * j + 4, :], gates[:, 4 * j:4 * j + 4, :], ACT.Sigmoid).then_inc(sig, 1)
                for m in range(8):
                    s = (U_OUT + m) % 2
                    act.wait_ge(unit_done, U_OUT + m + 1)
                    if m >= 2:
                        act.wait_ge(m_step, 5 * (m - 1))
                    nc.scalar.activation(y_both[:, m % 2, :, :], ps[:, 2 * s:2 * s + 2, :], ACT.Copy).then_inc(branch, 1)

            @block.vector
            def _(dve):
                for j in range(4):
                    dve.wait_ge(at_h, j + 1)
                    nc.vector.tensor_tensor(at_lo[:, j, :], ps[:, 4 + j, :], at_hi[:, j, :].bitcast(F32), ALU.subtract).then_inc(at_l, 1)
                dve.wait_ge(sig, 4)
                for m in range(8):
                    n = 5 * m
                    dve.wait_ge(branch, m + 1)
                    nc.vector.tensor_tensor(m_t[:, 0, :], y_both[:, m % 2, 0, :], gates[:, m, :], ALU.mult).then_inc(m_step, 1)
                    nc.vector.tensor_tensor(m_t[:, 1, :], y_both[:, m % 2, 1, :], gates[:, 8 + m, :], ALU.mult).then_inc(m_step, 1)
                    dve.wait_ge(m_step, n + 2)
                    nc.vector.tensor_tensor(m_t[:, 2, :], m_t[:, 0, :], m_t[:, 1, :], ALU.add).then_inc(m_step, 1)
                    dve.wait_ge(m_step, n + 3)
                    nc.vector.tensor_copy(mix_hi[:, m, :], m_t[:, 2, :]).then_inc(m_step, 1)
                    dve.wait_ge(m_step, n + 4)
                    nc.vector.tensor_tensor(mix_lo[:, m, :], m_t[:, 2, :], mix_hi[:, m, :].bitcast(F32), ALU.subtract).then_inc(m_step, 1)
                    dve.wait_ge(m_step, n + 5)

        x1_done = sem("x1_done")
        norm_ffn = Norm(lambda j: xT[:, j, 0:T1], KD, HALVES1, D, lambda j: prm("g_ffn", j), 6, 130, slots=4)
        put = region(0)
        h2_hi = put("h2_hi", [P, KD, T1], F32R)
        h2_lo = put("h2_lo", [P, KD, T1], F32R)
        h2_parts = (lambda j: h2_hi[:, j, :]), (lambda j: h2_lo[:, j, :])
        w_up = io["w_up"][0]

        def up_cols(j):
            return (j // 2) * P + (j % 2) * FFN

        with nc.Block() as block:
            mix_x = x_parts(mix_hi, mix_lo)

            @block.sync
            def _(sp):
                with sp.Fori(0, 3) as i:
                    for e in range(2):
                        u = U_O + 2 + e
                        load_unit(sp, 2 * i + u, u % 2, wcols_at(w_o, 256 * i + P * (2 + e)))
                for j in range(2):
                    load_unit(sp, U_UP + j, (U_UP + j) % 2, wcols(w_up, up_cols(j)))

            @block.gpsimd
            def _(pool):
                with pool.Fori(0, 4) as i:
                    for e in range(2):
                        u = U_O + 2 + e
                        split_unit(pool, 2 * i + u, u % 2)
                norm_ffn.pool_parts(pool, *h2_parts, 8)

            @block.tensor
            def _(pe):
                for m in range(8):
                    u = U_O + m
                    pe.wait_ge(split_ready, u + 1)
                    if m >= 2:
                        pe.wait_ge(x1_done, m - 1)
                    for k in range(KD):
                        mm = product(ps[:, u % 2, :], block_of(u % 2, k), mix_x(k), k == 0, k == KD - 1)
                    mm.then_inc(unit_done, 1)
                norm_ffn.pe(pe)

            @block.scalar
            def _(act):
                norm_ffn.act(act, lambda e, j: e.wait_ge(x1_done, j + 1))
                norm_ffn.act_parts(act, h2_parts[0], 8)

            @block.vector
            def _(dve):
                dve.wait_ge(s_x, 32)
                for m in range(8):
                    dve.wait_ge(unit_done, U_O + m + 1)
                    nc.vector.tensor_tensor(xT[:, m, 0:T1], xT[:, m, 0:T1], ps[:, (U_O + m) % 2, :], ALU.add).then_inc(x1_done, 1)
                dve.wait_ge(x1_done, 8)
                norm_ffn.dve_parts(dve, *h2_parts)

        put = region(32)
        act_hi = put("act_hi", [P, KF, T1], F32R)
        act_lo = put("act_lo", [P, KF, T1], F32R)
        up_raw = put("up_raw", [P, 2, T1 + 2])
        up_c = put("up_c", [P, 2, 3, T1])
        up_silu = put("up_silu", [P, T1])
        up_prod = put("up_prod", [P, T1])
        up_out = sem("up_out")
        up_w2 = sem("up_w2")
        taps = sem("taps")
        up_gate = sem("up_gate")
        up_step = sem("up_step")
        w_down = io["w_down"][0].rearrange("(k p) n -> p k n", p=P)

        def down_src(j, half):
            return w_down[:, 2 * j:2 * j + 2, 512 * half:512 * half + 512]

        with nc.Block() as block:
            @block.sync
            def _(sp):
                with sp.Fori(1, KF) as i:
                    for ab in range(2):
                        load_unit(sp, 2 * i + (U_UP + ab), (U_UP + ab) % 2, wcols_at(w_up, P * i + FFN * ab))
                for e in range(2):
                    load_unit(sp, U_DOWN + e, (U_DOWN + e) % 2, down_src(0, e))

            @block.gpsimd
            def _(pool):
                with pool.Fori(1, KF + 1) as i:
                    for ab in range(2):
                        split_unit(pool, 2 * i + (U_UP + ab), (U_UP + ab) % 2)

            @block.tensor
            def _(pe):
                with pe.Fori(0, KF) as i:
                    for ab in range(2):
                        s = (U_UP + ab) % 2
                        pe.wait_ge(split_ready, 2 * i + (U_UP + ab + 1))
                        pe.wait_ge(up_out, 2 * i + ab)
                        for k in range(KD):
                            mm = product(ps[:, s, :], block_of(s, k), (h2_hi[:, k, :], h2_lo[:, k, :]), k == 0, k == KD - 1)
                        mm.then_inc(unit_done, 1)

            @block.scalar
            def _(act):
                act.sem_inc(up_out, 1)
                with act.Fori(0, KF) as i:
                    for ab in range(2):
                        act.wait_ge(unit_done, 2 * i + (U_UP + ab + 1))
                        act.wait_ge(taps, 4 * i + (2 * ab + 2))
                        nc.scalar.activation(up_raw[:, ab, 2:2 + T1], ps[:, (U_UP + ab) % 2, :], ACT.Copy).then_inc(up_out, 1)
                        act.wait_ge(up_out, 2 * i + (ab + 2))
                        nc.scalar.activation(up_c[:, ab, 0, :], up_raw[:, ab, 2:2 + T1], ACT.Copy,
                                             scale=prm_at("cf2", i + KF * ab)).then_inc(up_w2, 1)
                    act.wait_ge(taps, 4 * i + 6)
                    act.wait_ge(up_step, 3 * i)
                    nc.scalar.activation(up_silu[:], up_c[:, 0, 2, :], ACT.Silu).then_inc(up_gate, 1)

            @block.vector
            def _(dve):
                for ab in range(2):
                    nc.vector.memset(up_raw[:, ab, 0:2], 0.0).then_inc(taps, 2)
                dve.wait_ge(taps, 4)
                with dve.Fori(0, KF) as i:
                    dve.wait_ge(up_gate, i)
                    for ab in range(2):
                        dve.wait_ge(up_w2, 2 * i + (ab + 1))
                        for k in range(2):
                            nc.vector.scalar_tensor_tensor(
                                out=up_c[:, ab, 1 + k, :], in0=up_raw[:, ab, 1 - k:1 - k + T1],
                                scalar=prm_at(("cf1", "cf0")[k], i + KF * ab), in1=up_c[:, ab, k, :],
                                op0=ALU.mult, op1=ALU.add).then_inc(taps, 1)
                            dve.wait_ge(taps, 4 * i + (4 + 2 * ab + k + 1))
                    dve.wait_ge(up_gate, i + 1)
                    nc.vector.tensor_tensor(up_prod[:], up_silu[:], up_c[:, 1, 2, :], ALU.mult).then_inc(up_step, 1)
                    dve.wait_ge(up_step, 3 * i + 1)
                    nc.vector.tensor_copy(act_hi[:, bass.ds(i, 1), :], up_prod[:]).then_inc(up_step, 1)
                    dve.wait_ge(up_step, 3 * i + 2)
                    nc.vector.tensor_tensor(act_lo[:, bass.ds(i, 1), :], up_prod[:], act_hi[:, bass.ds(i, 1), :].bitcast(F32),
                                            ALU.subtract).then_inc(up_step, 1)

        put = region(0)
        x2T = put("x2T", [P, KD, T1])
        meta = put("meta", [N_META, D])
        x2_done = sem("x2_done")
        norm_f = Norm(lambda j: x2T[:, j, :], KD, HALVES1, D, lambda j: prm("g_f", j), 0, 125)
        norm_pre0 = Norm(lambda j: xT[:, j, :], KD, HALVES2, D, lambda j: prm("pre", j), 6, 105)
        put = region(139)
        lv_diag = put("lv_diag", [P, 7, C])
        put = region(146)
        g_mask = put("g_mask", [P, P])
        lv_mask = put("lv_mask", [P, 6, C])
        ident_2 = put("ident_2", [P, C])
        halves_ones = put("halves_ones", [P, P])
        restart = put("restart", [P, TP])
        cst2 = sem("cst2")
        s_meta = sem("s_meta")
        meta_turned = sem("meta_turned")
        meta_in = sem("meta_in")

        with nc.Block() as block:
            @block.sync
            def _(sp):
                sp.dma_start(meta[:], io["meta_tokens_2"]).then_inc(s_meta, 16)
                with sp.Fori(1, KF // 2) as j:
                    for e in range(2):
                        load_unit(sp, 2 * j + (U_DOWN + e), (U_DOWN + e) % 2,
                                  w_down[:, bass.ds(2 * j, 2), 512 * e:512 * e + 512])

            @block.gpsimd
            def _(pool):
                with pool.Fori(1, KF // 2) as j:
                    for e in range(2):
                        split_unit(pool, 2 * j + (U_DOWN + e), (U_DOWN + e) % 2)
                n = [0]

                def step(ins):
                    ins.then_inc(cst2, 1)
                    n[0] += 1
                    pool.wait_ge(cst2, n[0])

                step(nc.gpsimd.memset(halves_ones[:], 0.0))
                step(nc.gpsimd.memset(halves_ones[0:64, 0:64], 1.0))
                step(nc.gpsimd.memset(halves_ones[64:128, 64:128], 1.0))
                step(nc.gpsimd.memset(restart[:], 1.0))
                step(nc.gpsimd.memset(restart[:].rearrange("p (a b) -> p a b", b=C)[:, :, 0:1], 0.0))
                step(nc.gpsimd.memset(g_mask[:], 1.0))
                for half in (0, C):
                    for col, op in ((0, ALU.is_ge), (C, ALU.is_gt)):
                        m = g_mask[half:half + C, col:col + C]
                        step(nc.gpsimd.affine_select(out=m, in_=m, compare_op=op, fill=0.0, base=0,
                                                     pattern=[[1, C]], channel_multiplier=-1))
                step(nc.gpsimd.memset(lv_diag[:], 1.0))
                for lv in range(6):
                    b = 1 << lv
                    for half in (0, C):
                        m = lv_diag[half:half + C, lv, :].rearrange("p (a b) -> p a b", b=b)
                        step(nc.gpsimd.affine_select(out=m, in_=m, compare_op=ALU.is_ge, fill=0.0, base=0,
                                                     pattern=[[-b, C // b], [0, b]], channel_multiplier=1))
                        step(nc.gpsimd.affine_select(out=m, in_=m, compare_op=ALU.is_ge, fill=0.0, base=b - 1,
                                                     pattern=[[b, C // b], [0, b]], channel_multiplier=-1))
                step(nc.gpsimd.tensor_tensor(lv_mask[:], lv_diag[:, 1:7, :], lv_diag[:, 0:6, :], ALU.subtract))
                step(nc.gpsimd.tensor_tensor(ident_2[:], ident[:, 0:C], ident[:, C:P], ALU.add))

            @block.tensor
            def _(pe):
                def unit(j, e, start, stop):
                    s = (U_DOWN + e) % 2
                    pe.wait_ge(split_ready, 2 * j + (U_DOWN + e + 1))
                    for k in range(2):
                        x = tuple(a[:, 2 * j + k, :] for a in (act_hi, act_lo))
                        for m in range(4):
                            mm = product(ps[:, 4 * e + m, :], block_of(s, 4 * k + m), x, start and k == 0, stop and k == 1)
                    mm.then_inc(unit_done, 1)
                for e in range(2):
                    unit(0, e, True, False)
                with pe.Fori(1, KF // 2 - 1) as j:
                    for e in range(2):
                        unit(j, e, False, False)
                for e in range(2):
                    unit(KF // 2 - 1, e, False, True)
                norm_f.pe(pe)
                pe.wait_ge(s_meta, 16)
                for j in range(KD):
                    mm = nc.tensor.transpose(ps[:, 1, j * N_META:(j + 1) * N_META], meta[:, j * P:j * P + P],
                                             ident[0:N_META, 0:N_META])
                mm.then_inc(meta_turned, 1)
                norm_pre0.pe(pe)

            @block.scalar
            def _(act):
                def both_written(act, j):
                    act.wait_ge(meta_in, 1)
                    act.wait_ge(y_ready, norm_f.t0 + j + 1)
                norm_f.act(act, lambda e, j: e.wait_ge(x2_done, j + 1))
                norm_pre0.act(act, both_written)

            @block.vector
            def _(dve):
                dve.wait_ge(unit_done, U_DOWN + KF)
                for m in range(KD):
                    nc.vector.tensor_tensor(x2T[:, m, :], xT[:, m, 0:T1], ps[:, m, :], ALU.add).then_inc(x2_done, 1)
                dve.wait_ge(x2_done, KD)
                dve.wait_ge(meta_turned, 1)
                nc.vector.tensor_copy(xT[:, :, 0:N_META], ps[:, 1, 0:KD * N_META].rearrange("p (k n) -> p k n", k=KD)).then_inc(meta_in, 1)
                dve.wait_ge(meta_in, 1)
                norm_f.dve(dve, y=lambda j: xT[:, j, N_META:T2])

        put = region(-PARTS_KB)
        mixed = [put(f"mixed_{n}", [P, KD, T2]) for n in "rkvg"]
        KEEP = 46
        uT = put("uT", [P, KD, 1 + T2])
        dx = put("dx", [P, KD, T2])
        lora_w = put("lora_w", [P, KD, P])
        lora_mu = put("lora_mu", [P, KD, P])
        h_kept = nc.dram_tensor("h_kept", [P, KD, T2], F32, kind="Internal").ap()
        s_h = sem("s_h")
        s_lora = sem("s_lora")
        u_zero = sem("u_zero")
        dx_ready = sem("dx_ready")
        lora_scaled = sem("lora_scaled")
        lo_used = sem("lo_used")
        mx_scaled = sem("mx_scaled")
        mx_done = sem("mx_done")
        mx_pool = sem("mx_pool")
        lora_out = sem("lora_out")
        rw_landed = [sem(f"rw_landed{s}") for s in range(2)]
        rw_used = sem("rw_used")
        rw_in = io["rwkv_w_in_2"][0]
        rw_view = rw_in.rearrange("(k p) n -> p k n", p=P)
        raw_k = [r[:, 0:1024].rearrange("p (k n) -> p k n", k=KD) for r in raw]

        with nc.Block() as block:
            @block.sync
            def _(sp):
                sp.dma_start(lora_w[:], rw_view[:, :, 4 * DI:4 * DI + P]).then_inc(s_lora, 16)
                sp.dma_start(h_kept, xT[:]).then_inc(s_h, 16)
                for t in range(2):
                    sp.dma_start(raw_k[t], rw_view[:, :, DI * t:DI * t + P]).then_inc(rw_landed[t], 16)
                sp.wait_ge(s_h, 16)

            @block.gpsimd
            def _(pool):
                for t in (2, 3):
                    for j in range(KD):
                        q = KD * (t - 2) + j
                        pool.wait_ge(mx_scaled, q + 1)
                        nc.gpsimd.tensor_tensor(mixed[t][:, j, :], mixed[t][:, j, :], uT[:, j, 1:1 + T2],
                                                ALU.add).then_inc(mx_pool, 1)
                        pool.wait_ge(mx_pool, q + 1)

            @block.tensor
            def _(pe):
                pe.wait_ge(s_lora, 16)
                pe.wait_ge(lora_scaled, 2 * KD)
                for j in range(KD):
                    pe.wait_ge(y_ready, norm_pre0.t0 + j + 1)
                    for h, (at, n) in enumerate(HALVES2):
                        nc.tensor.matmul(ps[:, h, 0:n], lora_w[:, j, :], uT[:, j, 1 + at:1 + at + n], start=(j == 0), stop=False)
                    pe.wait_ge(dx_ready, j + 1)
                    for h, (at, n) in enumerate(HALVES2):
                        mm = nc.tensor.matmul(ps[:, h, 0:n], lora_mu[:, j, :], dx[:, j, at:at + n], start=False, stop=(j == KD - 1))
                mm.then_inc(lo_used, 1)

            @block.scalar
            def _(act):
                act.wait_ge(s_lora, 16)
                for j in range(KD):
                    for t in range(2):
                        nc.scalar.activation(lora_mu[:, j, 64 * t:64 * t + 64], lora_w[:, j, 64 * t:64 * t + 64], ACT.Copy,
                                             scale=prm("mu", 8 * (4 + t) + j)).then_inc(lora_scaled, 1)
                for t in (2, 3):
                    for j in range(KD):
                        act.wait_ge(dx_ready, j + 1)
                        nc.scalar.activation(mixed[t][:, j, :], dx[:, j, :], ACT.Copy,
                                             scale=prm("mu", 8 * t + j)).then_inc(mx_scaled, 1)
                act.wait_ge(lo_used, 1)
                halves = wa_in[:].rearrange("p (a b) -> p a b", a=2)
                nc.scalar.activation(halves[0:64], ps[0:64, 0:2, 0:T2 // 2], ACT.Tanh).then_inc(lora_out, 1)
                nc.scalar.activation(halves[64:128], ps[64:128, 0:2, 0:T2 // 2], ACT.Copy).then_inc(lora_out, 1)

            @block.vector
            def _(dve):
                nc.vector.memset(uT[:, :, 0:1], 0.0).then_inc(u_zero, 1)
                dve.wait_ge(u_zero, 1)
                norm_pre0.dve(dve, y=lambda j: uT[:, j, 1:1 + T2])
                for j in range(KD):
                    nc.vector.tensor_tensor(dx[:, j, :], uT[:, j, 0:T2], uT[:, j, 1:1 + T2], ALU.subtract).then_inc(dx_ready, 1)
                dve.wait_ge(dx_ready, KD)
                for t in range(2):
                    for j in range(KD):
                        nc.vector.scalar_tensor_tensor(out=mixed[t][:, j, :], in0=dx[:, j, :], scalar=prm("mu", 8 * t + j),
                                                       in1=uT[:, j, 1:1 + T2], op0=ALU.mult, op1=ALU.add).then_inc(mx_done, 1)
                dve.wait_ge(mx_done, 2 * KD)

        put = region(0)
        z_hi = put("z_hi", [P, PAIRS, T2], F32R)
        z_lo = put("z_lo", [P, PAIRS, T2], F32R)
        Z_END = put.end
        put = region(KEEP)
        r_b, k_b, v_b, g_b, gs_b, ws_b, a_b = (put(f"{n}_b", [P, TP]) for n in ("r", "k", "v", "g", "gs", "ws", "a"))
        ld, lsum, lx, e_in, e_ex, e_neg = (put(f"{n}", [P, TP]) for n in ("ld", "lsum", "lx", "e_in", "e_ex", "e_neg"))
        kp, kk_b, sq_b, an_b, rr_b, rn_b = (put(f"{n}", [P, TP]) for n in ("kp", "kk_b", "sq_b", "an_b", "rr_b", "rn_b"))
        assert put.end >= Z_END
        rkv = put("rkv", [P, NC_, 3 * C])
        bk = put("bk", [P, NC_, 2 * C])
        kk_c = put("kk_c", [P, NC_, C])
        r_c = put("r_c", [P, NC_, C])
        gm = put("gm", [P, 2 * NC_, P])
        t_m = put("t_m", [P, NC_, C])
        t_t = put("t_t", [P, NC_, C])
        x_m = put("x_m", [P, NC_, C])
        bk_rows = put("bk_rows", [P, NC_, P])
        uv = put("uv", [P, 2 * NC_, C])
        y_c = put("y_c", [P, TP])
        p_sb = put("p_sb", [P, C])
        s0e = put("s0e", [P, C])
        ec = put("ec", [P, NC_])
        ec_c = put("ec_c", [P, NC_])
        wa2 = put("wa2", [P, P])
        z_hl = put("z_hl", [P, 2, T2], F32R)
        sb_a, sb_c = xT[:, 0:2, :], xT[:, 2:4, :]
        yc_b, ysq_b, yn_b, yb_b = (xT[:, n, :] for n in range(4, 8))
        sb_kept = nc.dram_tensor("sb_kept", [PAIRS, P, 2, T2], F32, kind="Internal").ap()
        z_kept = nc.dram_tensor("z_kept", [PAIRS, P, 2, T2], F32, kind="Internal").ap()

        assert put.end <= 146, put.end
        s_wa = sem("s_wa")
        s_sbk = sem("s_sbk")
        s_sbl = sem("s_sbl")
        s_zk = sem("s_zk")
        a_mm = sem("a_mm")
        a_ev = sem("a_ev")
        pa = sem("pa")
        pp = sem("pp")
        scanned = sem("scanned")
        ssk_mm = sem("ssk_mm")
        ssk_out = sem("ssk_out")
        bon_mm = sem("bon_mm")
        turn_mm = sem("turn_mm")
        turn_ev = sem("turn_ev")
        kept_c = sem("kept_c")
        g_mm = sem("g_mm")
        g_ev = sem("g_ev")
        tr_ev = sem("tr_ev")
        x_mm, x_ev = sem("x_mm"), sem("x_ev")
        tt_mm, tt_ev = sem("tt_mm"), sem("tt_ev")
        tt0 = sem("tt0")
        p_mm, p_ev = sem("p_mm"), sem("p_ev")
        u_mm, u_ev = sem("u_mm"), sem("u_ev")
        s_mm, s_ev = sem("s_mm"), sem("s_ev")
        s0_ev = sem("s0_ev")
        state0 = sem("state0")
        yy_mm, yy_ev = sem("yy_mm"), sem("yy_ev")
        mean_mm, yc_ev, ysq_ev = sem("mean_mm"), sem("yc_ev"), sem("ysq_ev")
        gs_ev, v_ev = sem("gs_ev"), sem("v_ev")
        var_mm, gn_ln, gn_r, yn_ev, yb_ev = (sem(n) for n in ("var_mm", "gn_ln", "gn_r", "yn_ev", "yb_ev"))
        s_z = sem("s_z")
        z_pool, z_hi_ev, pads = sem("z_pool"), sem("z_hi_ev"), sem("pads")
        DECAY = -float(2.718281828459045 ** -0.5)
        PARTS = [(0, 3), (3, 3), (6, 3)]
        own = [slice(C * h, C * h + C) for h in range(2)]
        AFTER_X, AFTER_TT = (3, 3, 0, 0, 0), (2, 5, 0, 0, 0)
        TURNS = [(0, 4), (4, 4), (8, 1)]

        met_pe, met_act = sem("met_pe"), sem("met_act")

        def held(eng):
            eng.sem_inc(met_pe if eng is nc.tensor else met_act, 1)

        def ge(eng, s, v):
            if not (isinstance(v, int) and v <= 0):
                eng.wait_ge(s, v)

        def halves_of(buf, at=PAD):
            return buf[:, at:at + T2].rearrange("p (a b) -> p a b", a=2)

        def both_banks():
            return ps[:, 0:2, 0:T2 // 2]

        def token_cols(buf, h):
            return buf[:, PAD + h * (T2 // 2):PAD + (h + 1) * (T2 // 2)]

        ITEMS = [("r", 0), ("w", 0), ("r", 1), ("w", 1), ("k", 0), ("a", 0), ("k", 1), ("a", 1),
                 ("v", 0), ("v", 1), ("g", 0), ("g", 1)]
        ITEM_BANK = [4 if kind in "wa" else h for kind, h in ITEMS]
        ENDS_AT = {1: (0,), 2: (1,), 4: (2, 3), 6: (4, 5), 8: (6, 7)}

        def a_products(pe, i, n, after_mean):
            kind, h = ITEMS[n]
            bank = ITEM_BANK[n]
            cols = slice(h * (T2 // 2), (h + 1) * (T2 // 2))
            dst = ps[:, bank, 0:T2 // 2]
            before = [m for m in range(n) if ITEM_BANK[m] == bank]
            if n == 0:
                ge(pe, pa, 14 * i - 2)
            elif before:
                pe.wait_ge(a_ev, 12 * i + (before[-1] + 1))
            if n == 8 and after_mean:
                pe.wait_ge(yc_ev, i - 1)
            if kind in "rkvg":
                t = "rkvg".index(kind)
                if h == 0:
                    pe.wait_ge(rw_landed[t % 2], 32 * i + (16 * (t // 2) + 16))
                for k in range(KD):
                    mm = nc.tensor.matmul(dst, raw_k[t % 2][:, k, :], mixed[t][:, k, cols], start=(k == 0), stop=(k == KD - 1))
                    if k == KD - 1:
                        mm.then_inc(a_mm, 1)
                    yield
            else:
                r = slice(0, 64) if kind == "w" else slice(64, 128)
                if n == 1:
                    pe.wait_ge(s_wa, 32 * i + 32)
                nc.tensor.matmul(dst, wa2[r, :], wa_in[r, cols], start=True, stop=True).then_inc(a_mm, 1)
                yield

        def pass_pe(pe, i, A, B, Cs):
            b, c = i - 1, i - 2
            if Cs:
                pe.wait_ge(tt_ev, 15 * c + 15)
                pe.wait_ge(kept_c, 5 * c + 5)
                pe.wait_ge(state0, 2 * c + 2)
            steps = itertools.chain.from_iterable(a_products(pe, i, item, Cs) for item in (range(8) if A else []))

            def fill(k):
                for _ in range(k):
                    next(steps, None)
            for n in range(NC_):
                if Cs:
                    pair = [h * NC_ + n for h in range(2)]
                    if n:
                        pe.wait_ge(s_ev, 16 * c + 2 * n)
                    held(pe)
                    for h, hc in enumerate(pair):
                        mm = nc.tensor.matmul(ps[own[h], 2, 0:C], gm[:, hc, C:P], uv[:, hc, :], start=True, stop=True)
                    mm.then_inc(p_mm, 1)
                    ge(pe, yy_ev, 18 * c + 2 * n)
                    held(pe)
                    for h, hc in enumerate(pair):
                        nc.tensor.matmul(ps[own[h], 5 + 2 * h, 0:C], uv[own[h], hc, :], r_c[own[h], n, :], start=True, stop=False)
                fill(1)
                if Cs:
                    pe.wait_ge(p_ev, 9 * c + (n + 1))
                    held(pe)
                    for h in range(2):
                        mm = nc.tensor.matmul(ps[own[h], 3 + 3 * h, 0:C], t_t[own[h], n, :], p_sb[own[h], :], start=True, stop=True)
                    mm.then_inc(u_mm, 1)
                fill(1)
                if Cs:
                    pe.wait_ge(u_ev, 18 * c + 2 * (n + 1))
                    if n < NC_ - 1:
                        for h, hc in enumerate(pair):
                            mm = nc.tensor.matmul(ps[own[h], 2, C:P], bk_rows[:, n, own[h]], uv[:, hc, :], start=True, stop=True)
                        mm.then_inc(s_mm, 1)
                    for h, hc in enumerate(pair):
                        mm = nc.tensor.matmul(ps[own[h], 5 + 2 * h, 0:C], uv[:, hc, :], gm[:, hc, 0:C], start=False, stop=True)
                    mm.then_inc(yy_mm, 1)
                fill(2)
            if Cs:
                pe.wait_ge(yy_ev, 18 * c + 18)
                ge(pe, gn_ln, c)
                if A:
                    pe.wait_ge(a_ev, 12 * i + 8)
                else:
                    pe.wait_ge(pa, 14 * PAIRS - 2)
                for h in range(2):
                    mm = nc.tensor.matmul(ps[:, h, 0:T2 // 2], halves_ones[:], token_cols(y_c, h), start=True, stop=True)
                mm.then_inc(mean_mm, 1)
            steps = itertools.chain.from_iterable(a_products(pe, i, item, Cs) for item in (range(8, 12) if A else []))
            if B:
                pe.wait_ge(pa, 14 * b + 14)
                pe.wait_ge(pp, 13 * b + 11)
                if A and not Cs:
                    pe.wait_ge(a_ev, 12 * i + 8)
                held(pe)
                for x in range(NC_):
                    for h in range(2):
                        mm = nc.tensor.matmul(ps[own[1 - h], 5 + x // 8, C * (x % 8):C * (x % 8) + C], rkv[:, x, 2 * C:3 * C],
                                              ident[:, own[h]], start=True, stop=True)
                mm.then_inc(turn_mm, 1)
                for q, (c0, m) in enumerate(TURNS):
                    for x in range(m):
                        mm = nc.tensor.transpose(ps[:, 2 + q, x * P:x * P + P], bk[:, c0 + x, :], ident[:])
                    mm.then_inc(turn_mm, 1)
                fill(8)
                for q, (c0, m) in enumerate(TURNS):
                    pe.wait_ge(turn_ev, 5 * b + (q + 3))
                    held(pe)
                    for x in range(m):
                        for h in range(2):
                            mm = nc.tensor.matmul(ps[:, 2 + 3 * h + q, x * P:x * P + P], bk[own[h], c0 + x, :],
                                                  rkv[own[h], c0 + x, 0:2 * C], start=True, stop=True)
                    mm.then_inc(g_mm, 1)

                fill(8)

                def part(bank, lhs, rhs, c0, m):
                    held(pe)
                    for x in range(m):
                        for h in range(2):
                            mm = nc.tensor.matmul(ps[own[h], bank + h, x * C:x * C + C], lhs(own[h], h, c0 + x), rhs(own[h], c0 + x),
                                                  start=True, stop=True)
                    return mm

                def level(lv):
                    for q, (c0, m) in enumerate(PARTS):
                        pe.wait_ge(tr_ev, 15 * b + (3 * lv - 3 + q + 1))
                        part(2 + 2 * q, lambda p, h, x: gm[p, h * NC_ + x, C:P], lambda p, x: t_m[p, x, :], c0, m).then_inc(x_mm, 1)
                    fill(AFTER_X[lv - 1])
                    for q, (c0, m) in enumerate(PARTS):
                        pe.wait_ge(x_ev, 15 * b + (3 * lv - 3 + q + 1))
                        part(2 + 2 * q, lambda p, h, x: x_m[p, x, :], lambda p, x: t_t[p, x, :], c0, m).then_inc(tt_mm, 1)
                fill(3)
                for lv in range(1, 6):
                    level(lv)
                    fill(AFTER_TT[lv - 1])
                    if lv == 2:
                        fill(2 * KD)
                        if Cs:
                            gn_var(pe, c, i, A)
                    if lv == 3 and A:
                        ssk(pe, i, Cs, c)
                if A:
                    bonus(pe, i)
            else:
                fill(4 * KD)
                if Cs:
                    gn_var(pe, c, i, A)
                if A:
                    ssk(pe, i, Cs, c)
                    bonus(pe, i)

        def chunks_of(bank, h, m):
            return ps[own[h], bank, 0:m * C].rearrange("p (a b) -> p a b", b=C)

        def gn_var(pe, c, i, after_items):
            pe.wait_ge(ysq_ev, c + 1)
            if after_items:
                pe.wait_ge(a_ev, 12 * i + 12)
            for h in range(2):
                mm = nc.tensor.matmul(ps[:, h, 0:T2 // 2], halves_ones[:], ysq_b[:, h * (T2 // 2):(h + 1) * (T2 // 2)],
                                      start=True, stop=True)
            mm.then_inc(var_mm, 1)

        def ssk(pe, i, after_var, c):
            if after_var:
                pe.wait_ge(gn_ln, c + 1)
            else:
                pe.wait_ge(a_ev, 12 * i + 12)
            pe.wait_ge(pa, 14 * i + 6)
            for h in range(2):
                mm = nc.tensor.matmul(ps[:, h, 0:T2 // 2], halves_ones[:], token_cols(sq_b, h), start=True, stop=True)
            mm.then_inc(ssk_mm, 1)

        def bonus(pe, i):
            pe.wait_ge(ssk_out, i + 1)
            pe.wait_ge(pp, 13 * i + 2)
            for h in range(2):
                mm = nc.tensor.matmul(ps[:, h, 0:T2 // 2], halves_ones[:], token_cols(rr_b, h), start=True, stop=True)
            mm.then_inc(bon_mm, 1)

        def pass_act(act, i, A, B, Cs):
            b, c = i - 1, i - 2
            def item(n):
                kind, h = ITEMS[n]
                act.wait_ge(a_mm, 12 * i + (n + 1))
                if n == 0:
                    ge(act, pp, 13 * i - 9)
                if n == 8:
                    ge(act, pp, 13 * i)
                src = ps[:, ITEM_BANK[n], 0:T2 // 2]
                dst = {"r": r_b, "k": k_b, "v": v_b, "w": ws_b, "a": a_b, "g": g_b}[kind]
                if kind in "wa":
                    held(act)
                    nc.scalar.activation(token_cols(dst, h), src, ACT.Sigmoid, bias=prm_at(kind + "0", i)).then_inc(a_ev, 1)
                elif kind == "g":
                    nc.scalar.activation(token_cols(gs_b, h), src, ACT.Sigmoid).then_inc(gs_ev, 1)
                    nc.scalar.activation(token_cols(dst, h), src, ACT.Copy).then_inc(a_ev, 1)
                else:
                    nc.scalar.activation(token_cols(dst, h), src, ACT.Copy).then_inc(a_ev, 1)

            for n in range(NC_):
                if Cs:
                    if 1 <= n < NC_ - 1:
                        act.wait_ge(s_ev, 16 * c + 2 * n)
                        for h in range(2):
                            nc.scalar.activation(s0e[own[h], :], uv[own[h], h * NC_ + n, :], ACT.Copy,
                                                 scale=ec_c[own[h], n:n + 1]).then_inc(s0_ev, 1)
                    act.wait_ge(yy_mm, 9 * c + (n + 1))
                    if n == 0:
                        ge(act, yc_ev, c)
                    for h in range(2):
                        nc.scalar.activation(y_c[own[h], n * C:n * C + C], ps[own[h], 5 + 2 * h, 0:C], ACT.Copy).then_inc(yy_ev, 1)
                if A:
                    for k in ENDS_AT.get(n, ()):
                        item(k)

            def turned():
                act.wait_ge(turn_mm, 4 * b + 1)
                v_rows_of = ps[:, 5:7, :].rearrange("p a b -> p (a b)")[:, 0:NC_ * C].rearrange("p (a b) -> p a b", b=C)
                for h in range(2):
                    nc.scalar.activation(uv[own[1 - h], h * NC_:(h + 1) * NC_, :], v_rows_of[own[1 - h], :, :], ACT.Copy).then_inc(turn_ev, 1)
                for q, (c0, m) in enumerate(TURNS):
                    act.wait_ge(turn_mm, 4 * b + (q + 2))
                    nc.scalar.activation(bk_rows[:, c0:c0 + m, :], ps[:, 2 + q, 0:m * P].rearrange("p (a b) -> p a b", b=P),
                                         ACT.Copy).then_inc(turn_ev, 1)
                nc.scalar.activation(r_c[:], rkv[:, :, 0:C], ACT.Copy).then_inc(kept_c, 1)
                nc.scalar.activation(kk_c[:], rkv[:, :, C:2 * C], ACT.Copy).then_inc(kept_c, 1)
                nc.scalar.activation(ec_c[:], ec[:], ACT.Copy).then_inc(kept_c, 1)

            def kk_kept():
                act.wait_ge(kept_c, 5 * b + 3)
                act.wait_ge(x_mm, 15 * b + 15)
                for h in range(2):
                    nc.scalar.activation(gm[own[h], h * NC_:(h + 1) * NC_, C:P], kk_c[own[h], :, :], ACT.Copy).then_inc(kept_c, 1)

            def factors_1():
                ge(act, ssk_out, i)
                act.wait_ge(a_ev, 12 * i + 8)
                ge(act, bon_mm, i)
                nc.scalar.activation(ld[:, PAD:TP], ws_b[:, PAD:TP], ACT.Copy, scale=DECAY).then_inc(pa, 1)
                nc.scalar.activation(an_b[:, PAD:TP], a_b[:, PAD:TP], ACT.Copy, scale=-1.0).then_inc(pa, 1)
                nc.scalar.activation(kp[:, PAD:TP], a_b[:, PAD:TP], ACT.Identity, scale=prm_at("k_a", i),
                                     bias=omka[:, ds1(i)]).then_inc(pa, 1)
                nc.scalar.activation(rr_b[:, PAD:TP], r_b[:, PAD:TP], ACT.Copy, scale=prm_at("r_k", i)).then_inc(pa, 1)
                nc.scalar.activation(kk_b[:, PAD:TP], k_b[:, PAD:TP], ACT.Copy, scale=prm_at("k_k", i)).then_inc(pa, 1)
                nc.scalar.activation(sq_b[:, PAD:TP], k_b[:, PAD:TP], ACT.Square, scale=prm_at("k_k", i)).then_inc(pa, 1)

            def factors_2():
                act.wait_ge(scanned, i + 1)
                act.wait_ge(pp, 13 * i + 3)
                nc.scalar.activation(e_in[:], lsum[:], ACT.Exp).then_inc(pa, 1)
                nc.scalar.activation(e_ex[:], lx[:], ACT.Exp).then_inc(pa, 1)
                nc.scalar.activation(e_neg[:], lsum[:], ACT.Exp, scale=-1.0).then_inc(pa, 1)

            def factors_3():
                act.wait_ge(ssk_out, i + 1)
                nc.scalar.activation(halves_of(rn_b), halves_of(rn_b), ACT.Ln).then_inc(pa, 1)
                act.wait_ge(pa, 14 * i + 10)
                nc.scalar.activation(rn_b[:, PAD:TP], rn_b[:, PAD:TP], ACT.Exp, scale=-0.5).then_inc(pa, 1)

            def factors_4():
                act.wait_ge(bon_mm, i + 1)
                nc.scalar.activation(halves_of(sq_b), both_banks(), ACT.Copy).then_inc(pa, 1)
                ge(act, g_mm, 3 * i)
                act.wait_ge(a_ev, 12 * i + 12)
                nc.scalar.activation(rkv[:, 0, 3 * C - (C - PAD):3 * C], v_b[:, PAD:C], ACT.Copy).then_inc(pa, 1)
                nc.scalar.activation(rkv[:, 1:NC_, 2 * C:3 * C], v_b[:, C:TP].rearrange("p (a b) -> p a b", b=C),
                                     ACT.Copy).then_inc(v_ev, 1)
                act.wait_ge(v_ev, i + 1)
                act.wait_ge(pa, 14 * i + 9)
                nc.scalar.activation(ec[:], e_in[:].rearrange("p (a b) -> p a b", b=C)[:, :, C - 1], ACT.Copy).then_inc(pa, 1)

            def gn_square():
                act.wait_ge(yc_ev, c + 1)
                nc.scalar.activation(ysq_b, yc_b, ACT.Square).then_inc(ysq_ev, 1)

            def gn_rs():
                act.wait_ge(var_mm, c + 1)
                ge(act, z_pool, 3 * c)
                nc.scalar.activation(yb_b.rearrange("p (a b) -> p a b", a=2), both_banks(), ACT.Ln, scale=1.0 / 64,
                                     bias=eps_col[:, 1:2]).then_inc(gn_ln, 1)
                act.wait_ge(gn_ln, c + 1)
                nc.scalar.activation(ysq_b, yb_b, ACT.Exp, scale=-0.5).then_inc(gn_r, 1)

            def gn_affine():
                act.wait_ge(yn_ev, c + 1)
                ge(act, z_pool, 3 * c)
                nc.scalar.activation(yb_b, yn_b, ACT.Identity, scale=prm_at("ln_w", c), bias=prm_at("ln_b", c)).then_inc(yb_ev, 1)

            def z_upper():
                act.wait_ge(z_pool, 3 * c + 2)
                ge(act, s_zk, 16 * c)
                nc.scalar.activation(z_hl[:, 0, :], yn_b, ACT.Copy).then_inc(z_hi_ev, 1)

            if B:
                turned()
            if A:
                item(8)
                factors_1()
                item(9)
            if Cs:
                gn_square()
            if A:
                factors_2()
                item(10)
            if A:
                item(11)
            if Cs:
                gn_rs()
            if A:
                factors_3()
            if Cs:
                gn_affine()
            if B:
                kk_kept()
            if A:
                factors_4()
            if Cs:
                z_upper()

        def pass_dve(dve, i, A, B, Cs):
            b, c = i - 1, i - 2

            def turn_t(q):
                c0, m = PARTS[q]
                nc.vector.transpose(t_m[:, c0:c0 + m, :], t_t[:, c0:c0 + m, :]).then_inc(tr_ev, 1)
            if Cs:
                for n in range(NC_):
                    dve.wait_ge(p_mm, 9 * c + (n + 1))
                    nc.vector.tensor_copy(p_sb[:], ps[:, 2, 0:C]).then_inc(p_ev, 1)
                    if 1 <= n < NC_ - 1:
                        dve.wait_ge(s0_ev, 14 * c + 2 * n)
                    dve.wait_ge(u_mm, 9 * c + (n + 1))
                    for h in range(2):
                        nc.vector.tensor_copy(uv[own[h], h * NC_ + n, :], ps[own[h], 3 + 3 * h, 0:C]).then_inc(u_ev, 1)
                    if n < NC_ - 1:
                        if n == 0:
                            dve.wait_ge(kept_c, 5 * c + 5)
                        dve.wait_ge(s_mm, 8 * c + (n + 1))
                        for h in range(2):
                            new, add = uv[own[h], h * NC_ + n + 1, :], ps[own[h], 2, C:P]
                            if n == 0:
                                nc.vector.tensor_scalar(new, add, ec_c[own[h], 0:1], None, ALU.mult).then_inc(s_ev, 1)
                            else:
                                nc.vector.scalar_tensor_tensor(out=new, in0=add, scalar=ec_c[own[h], n:n + 1], in1=s0e[own[h], :],
                                                               op0=ALU.mult, op1=ALU.add).then_inc(s_ev, 1)
            if Cs:
                dve.wait_ge(mean_mm, c + 1)
                ge(dve, yn_ev, c)
                nc.vector.scalar_tensor_tensor(out=yc_b.rearrange("p (a b) -> p a b", a=2), in0=both_banks(), scalar=-1.0 / 64,
                                               in1=halves_of(y_c), op0=ALU.mult, op1=ALU.add).then_inc(yc_ev, 1)
            if B:
                for q, (c0, m) in enumerate(TURNS):
                    dve.wait_ge(g_mm, 3 * b + (q + 1))
                    for h in range(2):
                        nc.vector.tensor_tensor(gm[:, h * NC_ + c0:h * NC_ + c0 + m, :],
                                                ps[:, 2 + 3 * h + q, 0:m * P].rearrange("p (a b) -> p a b", b=P),
                                                g_mask[:].unsqueeze(1).to_broadcast([P, m, P]), ALU.mult).then_inc(g_ev, 1)
                for h in range(2):
                    nc.vector.memset(uv[own[h], h * NC_, :], 0.0).then_inc(state0, 1)
                dve.wait_ge(g_ev, 6 * b + 6)
                for h in range(2):
                    nc.vector.tensor_tensor(t_t[own[h], :, :], gm[own[h], h * NC_:(h + 1) * NC_, C:P],
                                            lv_mask[own[h], 0, :].unsqueeze(1).to_broadcast([C, NC_, C]), ALU.mult).then_inc(tt0, 1)
                dve.wait_ge(tt0, 5 * b + 2)
                for c0, m in PARTS:
                    nc.vector.tensor_tensor(t_t[:, c0:c0 + m, :], t_t[:, c0:c0 + m, :],
                                            ident_2[:].unsqueeze(1).to_broadcast([P, m, C]), ALU.add).then_inc(tt0, 1)
                for q in range(len(PARTS)):
                    dve.wait_ge(tt0, 5 * b + (q + 3))
                    turn_t(q)
            if A:
                dve.wait_ge(pa, 14 * i + 1)
                ge(dve, pa, 14 * i)
                nc.vector.tensor_tensor_scan(lsum[:], restart[:], ld[:], 0.0, ALU.mult, ALU.add).then_inc(scanned, 1)

            def level(lv):
                for q, (c0, m) in enumerate(PARTS):
                    dve.wait_ge(x_mm, 15 * b + (3 * lv - 3 + q + 1))
                    for h in range(2):
                        ins = nc.vector.tensor_tensor(x_m[own[h], c0:c0 + m, :], chunks_of(2 + 2 * q + h, h, m),
                                                      lv_mask[own[h], lv, :].unsqueeze(1).to_broadcast([C, m, C]), ALU.mult)
                    ins.then_inc(x_ev, 1)
                for q, (c0, m) in enumerate(PARTS):
                    dve.wait_ge(tt_mm, 15 * b + (3 * lv - 3 + q + 1))
                    if lv == 1:
                        dve.wait_ge(tt0, 5 * b + 5)
                    else:
                        dve.wait_ge(tt_ev, 15 * b + (3 * lv - 6 + q + 1))
                    for h in range(2):
                        ins = nc.vector.tensor_tensor(t_t[own[h], c0:c0 + m, :], chunks_of(2 + 2 * q + h, h, m),
                                                      t_t[own[h], c0:c0 + m, :], ALU.add)
                    ins.then_inc(tt_ev, 1)
                    if lv < 5:
                        dve.wait_ge(tt_ev, 15 * b + (3 * lv - 3 + q + 1))
                        turn_t(q)
            if B:
                level(1)
                level(2)
                level(3)
            if A:
                dve.wait_ge(ssk_mm, i + 1)
                ge(dve, pp, 13 * i)
                nc.vector.tensor_scalar(halves_of(rn_b), both_banks(), 1e-24, None, ALU.max).then_inc(ssk_out, 1)
            if B:
                level(4)
            if Cs:
                dve.wait_ge(gn_r, c + 1)
                dve.wait_ge(yc_ev, c + 1)
                ge(dve, z_pool, 3 * c)
                ge(dve, z_hi_ev, c)
                nc.vector.tensor_tensor(yn_b, yc_b, ysq_b, ALU.mult).then_inc(yn_ev, 1)
            if B:
                level(5)

        def pass_pool(pool, i, A, B, Cs):
            c = i - 2
            chunks = lambda buf: buf[:].rearrange("p (a b) -> p a b", b=C)

            def mul(dst, x, y, n, op=ALU.mult):
                nc.gpsimd.tensor_tensor(dst, x, y, op).then_inc(pp, 1)
                pool.wait_ge(pp, 13 * i + n)
            if A:
                t = slice(PAD, TP)
                pool.wait_ge(pa, 14 * i + 6)
                ge(pool, s_sbk, 16 * i)
                mul(kp[:, t], k_b[:, t], kp[:, t], 1)
                mul(rr_b[:, t], rr_b[:, t], kp[:, t], 2)
                pool.wait_ge(scanned, i + 1)
                mul(lx[:], lsum[:], ld[:], 3, ALU.subtract)
                pool.wait_ge(pa, 14 * i + 9)
                ge(pool, g_mm, 3 * i)
                ge(pool, kept_c, 5 * i - 2)
                mul(rkv[:, :, 0:C], chunks(r_b), chunks(e_in), 4)
                for h, at in ((0, C), (1, 0)):
                    mul(bk[own[h], :, at:at + C], chunks(kp)[own[h]], chunks(e_neg)[own[h]], 5 + h)
                pool.wait_ge(pa, 14 * i + 11)
                mul(kk_b[:, t], kk_b[:, t], rn_b[:, t], 7)
                mul(rkv[:, :, C:2 * C], chunks(kk_b), chunks(e_ex), 8)
                mul(an_b[:, t], kk_b[:, t], an_b[:, t], 9)
                for h, at in ((0, 0), (1, C)):
                    mul(bk[own[h], :, at:at + C], chunks(an_b)[own[h]], chunks(e_neg)[own[h]], 10 + h)
                pool.wait_ge(gs_ev, 2 * i + 2)
                pool.wait_ge(a_ev, 12 * i + 12)
                mul(sb_a[:, 0, :], g_b[:, t], gs_b[:, t], 12)
            if Cs:
                pool.wait_ge(yb_ev, c + 1)
                pool.wait_ge(s_sbl, 16 * c + 16)
                def step(ins, n):
                    ins.then_inc(z_pool, 1)
                    pool.wait_ge(z_pool, 3 * c + n)
                step(nc.gpsimd.tensor_tensor(yn_b, yb_b, sb_c[:, 1, :], ALU.add), 1)
                step(nc.gpsimd.tensor_tensor(yn_b, yn_b, sb_c[:, 0, :], ALU.mult), 2)
                pool.wait_ge(z_hi_ev, c + 1)
                step(nc.gpsimd.tensor_tensor(z_hl[:, 1, :], yn_b, z_hl[:, 0, :].bitcast(F32), ALU.subtract), 3)
            if A:
                pool.wait_ge(pa, 14 * i + 12)
                mul(sb_a[:, 1, :], v_b[:, slice(PAD, TP)], sq_b[:, slice(PAD, TP)], 13)

        U_WO, U_IN, U_H, U_MO = (UNITS[n][0] for n in ("wkv_out", "mla_in", "heads", "mla_out"))
        rw_out, mla_out = io["rwkv_w_out_2"][0], io["mla_w_out_2"][0]

        def out_src(w, c, half):
            cols = slice(c, c + P) if isinstance(c, int) else bass.ds(c, P)
            return w.rearrange("(k p) n -> p k n", p=P)[:, KD * half:KD * half + KD, cols]

        def load_z(sp, p0, n):
            for dst, part in ((z_hi, 0), (z_lo, 1)):
                sp.dma_start(dst[:, p0:p0 + n, :].bitcast(F32),
                             z_kept[p0:p0 + n, :, part, :].rearrange("a p n -> p a n")).then_inc(s_z, 16)

        def early_loads(sp):
            for s, n in ((a_mm, 12), (a_ev, 12), (pa, 14), (pp, 13), (scanned, 1), (ssk_mm, 1), (ssk_out, 1), (bon_mm, 1), (v_ev, 1)):
                sp.wait_ge(s, n * PAIRS)
            for n in range(2):
                load_unit(sp, U_WO + n, (U_WO + n) % 2, out_src(rw_out, 0, n))
            sp.wait_ge(s_zk, 16 * (PAIRS - 1))
            load_z(sp, 0, PAIRS - 1)

        def pass_sp(sp, i, A, B, Cs):
            c = i - 2
            if Cs:
                ge(sp, z_pool, 3 * c)
                sp.wait_ge(s_sbk, 16 * c + 16)
                sp.dma_start(sb_c, sb_kept[ds1(c), :, :, :].rearrange("a p b n -> p (a b) n")).then_inc(s_sbl, 16)
                if not (A or B):
                    early_loads(sp)
            if A:
                for t in (2, 3):
                    sp.wait_ge(a_mm, 12 * i + (3, 7)[t - 2])
                    sp.dma_start(raw_k[t % 2], rw_cols(DI * t, i)).then_inc(rw_landed[t % 2], 16)
            if A and not (isinstance(i, int) and i == PAIRS - 1):
                sp.wait_ge(a_mm, 12 * i + 8)
                load_wa(sp, i + 1)
                for t in (0, 1):
                    sp.wait_ge(a_mm, 12 * i + (10, 12)[t])
                    sp.dma_start(raw_k[t], rw_cols(DI * t, i + 1)).then_inc(rw_landed[t], 16)
            if Cs:
                sp.wait_ge(z_pool, 3 * c + 3)
                sp.dma_start(z_kept[ds1(c), :, :, :].rearrange("a p b n -> p (a b) n"), z_hl[:].bitcast(F32)).then_inc(s_zk, 16)
            if A:
                sp.wait_ge(pp, 13 * i + 13)
                sp.dma_start(sb_kept[ds1(i), :, :, :].rearrange("a p b n -> p (a b) n"), sb_a).then_inc(s_sbk, 16)

        def ds1(i):
            return slice(i, i + 1) if isinstance(i, int) else bass.ds(i, 1)

        def rw_cols(at, i):
            return rw_view[:, :, at + P * i:at + P * i + P] if isinstance(i, int) else rw_view[:, :, bass.ds(P * i + at, P)]

        def load_wa(sp, i):
            for r, w in ((0, io["rwkv_w2_2"][0]), (64, io["rwkv_a2_2"][0])):
                src = w[:, P * i:P * i + P] if isinstance(i, int) else w[:, bass.ds(P * i, P)]
                sp.dma_start(wa2[r:r + 64, :], src).then_inc(s_wa, 16)

        def all_passes(eng, body):
            body(eng, 0, True, False, False)
            body(eng, 1, True, True, False)
            with eng.Fori(2, PAIRS - 1) as i:
                body(eng, i, True, True, True)
            body(eng, PAIRS - 1, True, True, True)
            body(eng, PAIRS, False, True, True)
            body(eng, PAIRS + 1, False, False, True)

        with nc.Block() as block:
            @block.sync
            def _(sp):
                load_wa(sp, 0)
                all_passes(sp, pass_sp)
                sp.wait_ge(s_zk, 16 * PAIRS)

            @block.gpsimd
            def _(pool):
                pool.wait_ge(pads, 14)
                all_passes(pool, pass_pool)
                for n in range(2):
                    split_unit(pool, U_WO + n, (U_WO + n) % 2)

            @block.tensor
            def _(pe):
                all_passes(pe, pass_pe)

            @block.scalar
            def _(act):
                act.wait_ge(pads, 14)
                all_passes(act, pass_act)

            @block.vector
            def _(dve):
                for buf in (r_b, k_b, v_b, ld, kp, kk_b, an_b):
                    nc.vector.memset(buf[:, 0:PAD], 0.0).then_inc(pads, 1)
                nc.vector.memset(rkv[:, 0, 2 * C:3 * C], 0.0).then_inc(pads, 1)
                nc.vector.tensor_scalar(omka[:], prm("k_a", 0, 16), -1.0, 1.0, ALU.mult, ALU.add).then_inc(pads, 6)
                dve.wait_ge(pads, 14)
                all_passes(dve, pass_dve)

        put = region(68)
        mT = put("mT", [P, KD, T2])
        norm_post0 = Norm(lambda j: mT[:, j, :], KD, HALVES2, D, lambda j: prm("post", j), 6, 86)
        norm_pre1 = Norm(lambda j: xT[:, j, :], KD, HALVES2, D, lambda j: prm("pre", 8 + j), 6, 99, slots=4)
        put = region(117)
        u2_hi = put("u2_hi", [P, KD, T2], F32R)
        u2_lo = put("u2_lo", [P, KD, T2], F32R)
        u2_parts = (lambda j: u2_hi[:, j, :]), (lambda j: u2_lo[:, j, :])
        m_out = sem("m_out")
        h_added = sem("h_added")
        mla_in = io["mla_w_in_2"][0]
        IN_Q, IN_KV, IN_ROPE, IN_G = 0, 512, 768, 832
        in_cols = [IN_Q + P * m for m in range(4)] + [IN_KV, IN_KV + P, IN_ROPE]

        def out_products(pe, j, u0, e, x_of, parts, bank_free):
            for half in range(2):
                u = u0 + 2 * e + half
                pe.wait_ge(split_ready, 4 * j + (u + 1))
                if half == 0:
                    pe.wait_ge(bank_free, 2 * j + e)
                for k in range(KD):
                    for h, (at, n) in enumerate(parts):
                        mm = product(ps[:, len(parts) * e + h, 0:n], block_of(u % 2, k), x_of(KD * half + k, at, n),
                                     half == 0 and k == 0, half == 1 and k == KD - 1)
                mm.then_inc(unit_done, 1)

        with nc.Block() as block:
            @block.sync
            def _(sp):
                load_z(sp, PAIRS - 1, 1)
                for n in (2, 3):
                    load_unit(sp, U_WO + n, (U_WO + n) % 2, out_src(rw_out, P, n - 2))
                sp.dma_start(xT[:], h_kept).then_inc(s_h, 16)
                with sp.Fori(1, 4) as j:
                    for e in range(2):
                        for half in range(2):
                            u = U_WO + 2 * e + half
                            load_unit(sp, 4 * j + u, u % 2, out_src(rw_out, 256 * j + P * e, half))
                for n in range(2):
                    load_unit(sp, U_IN + n, (U_IN + n) % 2, wcols(mla_in, in_cols[n]))

            @block.gpsimd
            def _(pool):
                for n in (2, 3):
                    split_unit(pool, U_WO + n, (U_WO + n) % 2)
                with pool.Fori(1, 4) as j:
                    for n in range(4):
                        split_unit(pool, 4 * j + (U_WO + n), (U_WO + n) % 2)
                for n in range(2):
                    split_unit(pool, U_IN + n, (U_IN + n) % 2)
                norm_pre1.pool_parts(pool, *u2_parts, 16)

            @block.tensor
            def _(pe):
                pe.wait_ge(s_z, 64)
                with pe.Fori(0, 4) as j:
                    for e in range(2):
                        out_products(pe, j, U_WO, e, lambda k, at, n: (z_hi[:, k, at:at + n], z_lo[:, k, at:at + n]),
                                     HALVES2, m_out)
                norm_post0.pe(pe)
                norm_pre1.pe(pe)

            @block.scalar
            def _(act):
                norm_post0.act(act, lambda e, j: e.wait_ge(m_out, j + 2))
                norm_pre1.act(act, lambda e, j: e.wait_ge(h_added, j + 1))
                norm_pre1.act_parts(act, u2_parts[0], 16)

            @block.vector
            def _(dve):
                dve.sem_inc(m_out, 1)
                with dve.Fori(0, 4) as j:
                    for e in range(2):
                        dve.wait_ge(unit_done, 4 * j + (U_WO + 2 * e + 2))
                        nc.vector.tensor_copy(mT[:, bass.ds(2 * j + e, 1), :].rearrange("p o (a b) -> p (o a) b", a=2),
                                              ps[:, 2 * e:2 * e + 2, 0:T2 // 2]).then_inc(m_out, 1)
                dve.wait_ge(m_out, KD + 1)
                norm_post0.dve(dve, y=lambda j: mT[:, j, :])
                dve.wait_ge(s_h, 32)
                for j in range(KD):
                    nc.vector.tensor_tensor(xT[:, j, :], xT[:, j, :], mT[:, j, :], ALU.add).then_inc(h_added, 1)
                dve.wait_ge(h_added, KD)
                norm_pre1.dve_parts(dve, *u2_parts)

        put = region(0)
        gate = put("gate", [P, MH, T1])
        cq_hi, cq_lo = (put(n, [P, 4, T1], F32R) for n in ("cq_hi", "cq_lo"))
        ckv_hi, ckv_lo = (put(n, [P, 2, T2], F32R) for n in ("ckv_hi", "ckv_lo"))
        k_rot = put("k_rot", [ROPE, T2])
        cos_t, sin_t = put("cos_t", [ROPE, T2]), put("sin_t", [ROPE, T2])
        ATTN_KB = math.ceil(put.end)
        cq, ckv = put("cq", [P, 4, T1]), put("ckv", [P, 2, T2])
        k_x, k_sw = put("k_x", [ROPE, T2]), put("k_sw", [ROPE, T2])
        norm_q = Norm(lambda j: cq[:, j, :], 4, HALVES1, 512, lambda j: prm("qn", j), 2, 83)
        norm_kv = Norm(lambda j: ckv[:, j, :], 2, HALVES2, 256, lambda j: prm("kvn", j), 4, 98)
        s_tab = sem("s_tab")
        in_ev = sem("in_ev")
        k_step = sem("k_step")
        gate_ev = sem("gate_ev")
        q_up, kv_up = io["mla_w_q_up_2"][0], io["mla_w_kv_up_2"][0]
        QW = 128 + ROPE

        def load_head(sp, h, e):
            s = (U_H + e) % 2
            sp.wait_ge(split_ready, h + (U_H - 1))
            qc, kc = (slice(h * QW, h * QW + QW), slice(h * 256, h * 256 + 256)) if isinstance(h, int) else \
                (bass.ds(h * QW, QW), bass.ds(h * 256, 256))
            sp.dma_start(raw[s][:, 0:4 * QW].rearrange("p (k n) -> p k n", k=4),
                         q_up.rearrange("(k p) n -> p k n", p=P)[:, :, qc]).then_inc(half_in[s], 16)
            sp.dma_start(raw[s][:, 4 * QW:4 * QW + 512].rearrange("p (k n) -> p k n", k=2),
                         kv_up.rearrange("(k p) n -> p k n", p=P)[:, :, kc]).then_inc(landed[s], 16)

        def split_head(pool, i, e):
            pool.wait_ge(half_in[(U_H + e) % 2], 16 * i + 80)
            split_unit(pool, 2 * i + (U_H + e), (U_H + e) % 2, width=1280)

        with nc.Block() as block:
            @block.sync
            def _(sp):
                sp.dma_start(cos_t[:], io["rope_cos"]).then_inc(s_tab, 16)
                sp.dma_start(sin_t[:], io["rope_sin"]).then_inc(s_tab, 16)
                for n in range(2, 7):
                    load_unit(sp, U_IN + n, (U_IN + n) % 2, wcols(mla_in, in_cols[n]))
                with sp.Fori(0, MH // 2) as j:
                    for e in range(2):
                        load_unit(sp, 2 * j + (U_IN + 7 + e), (U_IN + 7 + e) % 2, wcols_at(mla_in, 256 * j + (IN_G + P * e)))
                for h in range(2):
                    load_head(sp, h, h)

            @block.gpsimd
            def _(pool):
                for n in range(2, 7):
                    split_unit(pool, U_IN + n, (U_IN + n) % 2)
                with pool.Fori(0, MH // 2) as j:
                    for e in range(2):
                        split_unit(pool, 2 * j + (U_IN + 7 + e), (U_IN + 7 + e) % 2)
                for h in range(2):
                    split_head(pool, 0, h)

            @block.tensor
            def _(pe):
                def unit(u, s, banks, parts):
                    pe.wait_ge(split_ready, u + 1)
                    for k in range(KD):
                        for b, (at, n) in zip(banks, parts):
                            mm = product(ps[:, b, 0:n], block_of(s, k), (u2_hi[:, k, at:at + n], u2_lo[:, k, at:at + n]),
                                         k == 0, k == KD - 1)
                    mm.then_inc(unit_done, 1)
                tail = [(N_META, T1)]
                for n, (banks, parts) in enumerate([((0,), tail), ((1,), tail), ((2,), tail), ((3,), tail),
                                                    ((4, 5), HALVES2), ((6, 7), HALVES2), ((0, 1), HALVES2)]):
                    if n == 6:
                        pe.wait_ge(in_ev, 2)
                    unit(U_IN + n, (U_IN + n) % 2, banks, parts)
                pe.wait_ge(in_ev, 6)
                norm_q.pe(pe)
                norm_kv.pe(pe)
                with pe.Fori(0, MH // 2) as j:
                    for e in range(2):
                        pe.wait_ge(gate_ev, 2 * j + e)
                        unit(2 * j + (U_IN + 7 + e), (U_IN + 7 + e) % 2, (6 + e,), tail)

            @block.scalar
            def _(act):
                for n in range(7):
                    act.wait_ge(unit_done, U_IN + n + 1)
                    two = lambda ap: ap.rearrange("p (a b) -> p a b", a=2)
                    if n < 4:
                        nc.scalar.activation(cq[:, n, :], ps[:, n, :], ACT.Copy).then_inc(in_ev, 1)
                    elif n < 6:
                        b = 4 + 2 * (n - 4)
                        nc.scalar.activation(two(ckv[:, n - 4, :]), ps[:, b:b + 2, 0:T2 // 2], ACT.Copy).then_inc(in_ev, 1)
                    else:
                        nc.scalar.activation(two(k_sw[0:32, :]), ps[32:64, 0:2, 0:T2 // 2], ACT.Copy)
                        nc.scalar.activation(two(k_sw[32:64, :]), ps[0:32, 0:2, 0:T2 // 2], ACT.Copy)
                        nc.scalar.activation(two(k_x[:]), ps[0:64, 0:2, 0:T2 // 2], ACT.Copy).then_inc(in_ev, 1)
                norm_q.act(act, lambda e, j: e.wait_ge(in_ev, j + 1))
                norm_kv.act(act, lambda e, j: e.wait_ge(in_ev, j + 5))
                act.sem_inc(gate_ev, 1)
                with act.Fori(0, MH // 2) as j:
                    for e in range(2):
                        act.wait_ge(unit_done, 2 * j + (U_IN + 8 + e))
                        held(act)
                        nc.scalar.activation(gate[:, bass.ds(2 * j + e, 1), :], ps[:, 6 + e:7 + e, :], ACT.Silu).then_inc(gate_ev, 1)

            @block.vector
            def _(dve):
                dve.wait_ge(in_ev, 7)
                dve.wait_ge(s_tab, 32)
                nc.vector.tensor_tensor(k_x[:], k_x[:], cos_t[:], ALU.mult).then_inc(k_step, 1)
                nc.vector.tensor_tensor(k_sw[:], k_sw[:], sin_t[:], ALU.mult).then_inc(k_step, 1)
                dve.wait_ge(k_step, 2)
                nc.vector.tensor_tensor(k_rot[:], k_x[:], k_sw[:], ALU.add).then_inc(k_step, 1)
                norm_q.dve(dve, hi=lambda j: cq_hi[:, j, :], lo=lambda j: cq_lo[:, j, :])
                norm_kv.dve(dve, hi=lambda j: ckv_hi[:, j, :], lo=lambda j: ckv_lo[:, j, :])
                dve.wait_ge(k_step, 3)

        put = region(ATTN_KB)
        z2_hi = put("z2_hi", [P, MH, T1], F32R)
        v_tok = put("v_tok", [P, 2, QB + 1, P])
        k_nope = put("k_nope", [P, 2, T2])
        q_nope = put("q_nope", [P, 2, T1])
        q_rot = put("q_rot", [ROPE, 2, T1])
        q_x, q_sw = put("q_x", [ROPE, T1]), put("q_sw", [ROPE, T1])
        prob = put("prob", [P, 2, T2])
        probT = put("probT", [P, QB + 1, T1])
        z_t = put("z_t", [P, T1])
        nmax, psum_r, prec = put("nmax", [P, 2]), put("psum_r", [P, 2]), put("prec", [P, 2])
        assert put.end <= 151
        up_mm = sem("up_mm")
        up_ev = sem("up_ev")
        q_step = sem("q_step")
        sc_mm = sem("sc_mm")
        sc_max = sem("sc_max")
        sc_exp = sem("sc_exp")
        sc_rec = sem("sc_rec")
        sc_norm = sem("sc_norm")
        pt_mm = sem("pt_mm")
        pt_ev = sem("pt_ev")
        oo_mm = sem("oo_mm")
        zt_ev = sem("zt_ev")
        zh_ev, zl_ev = sem("zh_ev"), sem("zl_ev")

        def keys(t):
            return N_META + P * (t + 1)

        def rows16(t):
            return slice(N_META + P * t, N_META + P * t + P)

        def head_cols(s, k, at, n=P):
            return tuple(w[s][:, QW * k + at:QW * k + at + n] for w in (w_hi, w_lo))

        def kv_cols(s, k, at, n=P):
            return tuple(w[s][:, 4 * QW + 256 * k + at:4 * QW + 256 * k + at + n] for w in (w_hi, w_lo))

        def up_item(pe, h, s, n):
            cq_of = lambda k: (cq_hi[:, k, :], cq_lo[:, k, :])
            if n == 0:
                pe.wait_ge(split_ready, h + (U_H + 1))
                pe.wait_ge(up_ev, 5 * h)
                for k in range(4):
                    mm = product(ps[:, 5, :], head_cols(s, k, 0), cq_of(k), k == 0, k == 3)
                mm.then_inc(up_mm, 1)
            elif n == 1:
                for k in range(4):
                    mm = product(ps[:, 6, :], head_cols(s, k, P), cq_of(k), k == 0, k == 3)
                mm.then_inc(up_mm, 1)
            elif n == 2:
                for part, (at, cols) in enumerate(HALVES2):
                    if part == 1:
                        pe.wait_ge(up_ev, 5 * h + 1)
                    for k in range(2):
                        mm = product(ps[:, (7, 5)[part], 0:cols], kv_cols(s, k, 0), (ckv_hi[:, k, at:at + cols], ckv_lo[:, k, at:at + cols]),
                                     k == 0, k == 1)
                    mm.then_inc(up_mm, 1)
            else:
                pe.wait_ge(up_ev, 5 * h + 3)
                for t in range(QB + 1):
                    at = 0 if t == 0 else N_META + P * (t - 1)
                    dst = ps[:, 7, 0:P] if t == 0 else ps[:, 6, P * (t - 1):P * t]
                    for k in range(2):
                        mm = product(dst, (ckv_hi[:, k, at:at + P], ckv_lo[:, k, at:at + P]), kv_cols(s, k, P), k == 0, k == 1)
                mm.then_inc(unit_done, 1)

        def up_out(act, h, s, n):
            if n == 0:
                act.wait_ge(up_mm, 4 * h + 1)
                nc.scalar.activation(q_nope[:, s, :], ps[:, 5, :], ACT.Copy, scale=MSCALE).then_inc(up_ev, 1)
            elif n == 1:
                act.wait_ge(up_mm, 4 * h + 2)
                act.wait_ge(q_step, 3 * h)
                nc.scalar.activation(q_sw[0:32, :], ps[32:64, 6, :], ACT.Copy, scale=MSCALE)
                nc.scalar.activation(q_sw[32:64, :], ps[0:32, 6, :], ACT.Copy, scale=MSCALE)
                nc.scalar.activation(q_x[:], ps[0:64, 6, :], ACT.Copy, scale=MSCALE).then_inc(up_ev, 1)
            elif n == 2:
                for part, (at, cols) in enumerate(HALVES2):
                    act.wait_ge(up_mm, 4 * h + (3 + part))
                    nc.scalar.activation(k_nope[:, s, at:at + cols], ps[:, (7, 5)[part], 0:cols], ACT.Copy).then_inc(up_ev, 1)
            else:
                act.wait_ge(unit_done, h + (U_H + 1))
                nc.scalar.activation(v_tok[0:N_META, s, 0, :], ps[0:N_META, 7, 0:P], ACT.Copy)
                nc.scalar.activation(v_tok[:, s, 1:QB + 1, :], ps[:, 6, :].rearrange("p (a b) -> p a b", b=P), ACT.Copy).then_inc(up_ev, 1)

        def rotate(dve, h, s):
            dve.wait_ge(up_ev, 5 * h + 2)
            tab = slice(N_META, T2)
            nc.vector.tensor_tensor(q_x[:], q_x[:], cos_t[:, tab], ALU.mult).then_inc(q_step, 1)
            nc.vector.tensor_tensor(q_sw[:], q_sw[:], sin_t[:, tab], ALU.mult).then_inc(q_step, 1)
            dve.wait_ge(q_step, 3 * h + 2)
            nc.vector.tensor_tensor(q_rot[:, s, :], q_x[:], q_sw[:], ALU.add).then_inc(q_step, 1)

        def score_banks(t, n):
            return [(0, n, t % 2)] if t < QB - 1 else [(0, T2 // 2, 0), (T2 // 2, T2 // 2, 1)]

        def scores_of(t):
            return ps[:, t % 2, 0:keys(t)] if t < QB - 1 else ps[:, 0:2, 0:T2 // 2]

        def values(pe, h, s):
            pe.wait_ge(pt_ev, 4 * h + 4)
            pe.wait_ge(zt_ev, h)
            nc.tensor.matmul(ps[:, 4, :], v_tok[0:N_META, s, 0, :], probT[0:N_META, 0, :], start=True, stop=False)
            for c in range(1, QB + 1):
                q = slice(P * (c - 1), T1)
                mm = nc.tensor.matmul(ps[:, 4, q], v_tok[:, s, c, :], probT[:, c, q], start=False, stop=(c == QB))
            mm.then_inc(oo_mm, 1)

        def gated(dve, h):
            dve.wait_ge(oo_mm, h + 1)
            dve.wait_ge(zl_ev, h)
            at = slice(h, h + 1) if isinstance(h, int) else bass.ds(h, 1)
            nc.vector.tensor_tensor(z_t[:].unsqueeze(1), ps[:, 4:5, :], gate[:, at, :], ALU.mult).then_inc(zt_ev, 1)
            dve.wait_ge(zt_ev, h + 1)
            nc.vector.tensor_copy(z2_hi[:, at, :], z_t[:].unsqueeze(1)).then_inc(zh_ev, 1)

        def all_heads(eng, body):
            for e in range(2):
                body(eng, 0, e, True)
            with eng.Fori(1, MH // 2 - 1) as i:
                for e in range(2):
                    body(eng, i, e, True)
            for e in range(2):
                body(eng, MH // 2 - 1, e, e == 0)

        def head_pe(pe, i, e, more):
            h = 2 * i + e
            def scores(t):
                if t == 0:
                    pe.wait_ge(up_ev, 5 * h + 5)
                    pe.wait_ge(q_step, 3 * h + 3)
                    pe.wait_ge(sc_exp, 4 * h)
                elif t >= 2:
                    pe.wait_ge(sc_exp, 4 * h + (t - 1 if t == 2 else 3))
                q = slice(P * t, P * t + P)
                for at, n, bank in score_banks(t, keys(t)):
                    diag = at + n == keys(t)
                    nc.tensor.matmul(ps[:, bank, 0:n], q_nope[:, e, q], k_nope[:, e, at:at + n], start=True, stop=False)
                    mm = nc.tensor.matmul(ps[:, bank, 0:n], q_rot[:, e, q], k_rot[:, at:at + n], start=False, stop=not diag)
                    if diag:
                        mm = nc.tensor.matmul(ps[:, bank, n - P:n], ident_b[:], causal_b[:], start=False, stop=True)
                mm.then_inc(sc_mm, 1)

            def turn(t):
                pe.wait_ge(sc_norm, 4 * h + (t + 1))
                if t < 2:
                    pe.wait_ge(pt_ev, 4 * h)
                else:
                    pe.wait_ge(pt_ev, 4 * h + (1 if t == 2 else 3))
                for c in range(1, t + 2):
                    nc.tensor.transpose(ps[:, 2 + t % 2, P * (c - 1):P * c], prob[:, t % 2, rows16(c - 1)], ident[:])
                meta_at = ps[0:N_META, 2 + t % 2, P * (t + 1):P * (t + 2)] if t < 3 else ps[0:N_META, 2, 0:P]
                nc.tensor.transpose(meta_at, prob[:, t % 2, 0:N_META], ident[:]).then_inc(pt_mm, 1)

            scores(0)
            scores(1)
            if not (isinstance(h, int) and h == 0):
                values(pe, h - 1, 1 - e)
            if more:
                up_item(pe, h + 1, 1 - e, 0)
            turn(0)
            scores(2)
            if more:
                up_item(pe, h + 1, 1 - e, 1)
            turn(1)
            scores(3)
            if more:
                up_item(pe, h + 1, 1 - e, 2)
            turn(2)
            if more:
                up_item(pe, h + 1, 1 - e, 3)
            turn(3)

        def head_act(act, i, e, more):
            h = 2 * i + e
            for t in range(QB):
                act.wait_ge(sc_max, 4 * h + (t + 1))
                act.wait_ge(pt_mm, 4 * h + (t - 1 if t >= 2 else 0))
                n = keys(t)
                dst = prob[:, t % 2, 0:n]
                if t == QB - 1:
                    dst = dst.rearrange("p (a b) -> p a b", a=2)
                nc.scalar.activation(dst, scores_of(t), ACT.Exp, bias=nmax[:, t % 2:t % 2 + 1],
                                     accum_out=psum_r[:, t % 2:t % 2 + 1]).then_inc(sc_exp, 1)
                if more and t:
                    up_out(act, h + 1, 1 - e, t - 1)
            if more:
                up_out(act, h + 1, 1 - e, 3)

        def head_dve(dve, i, e, more):
            h = 2 * i + e
            def maximum(t):
                dve.wait_ge(sc_mm, 4 * h + (t + 1))
                dve.wait_ge(sc_exp, 4 * h + (t - 1 if t >= 2 else 0))
                nc.vector.tensor_reduce(nmax[:, t % 2:t % 2 + 1], scores_of(t), AX_X if t < QB - 1 else AX_XY, ALU.max,
                                        negate=True).then_inc(sc_max, 1)

            def normalise(t):
                dve.wait_ge(sc_exp, 4 * h + (t + 1))
                nc.vector.reciprocal(prec[:, t % 2:t % 2 + 1], psum_r[:, t % 2:t % 2 + 1]).then_inc(sc_rec, 1)
                dve.wait_ge(sc_rec, 4 * h + (t + 1))
                p = prob[:, t % 2, 0:keys(t)]
                nc.vector.tensor_scalar(p, p, prec[:, t % 2:t % 2 + 1], None, ALU.mult).then_inc(sc_norm, 1)

            def turned_out(t):
                dve.wait_ge(pt_mm, 4 * h + (t + 1))
                dve.wait_ge(oo_mm, h)
                q = slice(P * t, P * t + P)
                meta_at = ps[0:N_META, 2 + t % 2, P * (t + 1):P * (t + 2)] if t < 3 else ps[0:N_META, 2, 0:P]
                nc.vector.tensor_copy(probT[0:N_META, 0, q], meta_at)
                nc.vector.tensor_copy(probT[:, 1:t + 2, q],
                                      ps[:, 2 + t % 2, 0:P * (t + 1)].rearrange("p (a b) -> p a b", b=P)).then_inc(pt_ev, 1)
            maximum(0)
            maximum(1)
            if not (isinstance(h, int) and h == 0):
                gated(dve, h - 1)
            normalise(0)
            turned_out(0)
            maximum(2)
            normalise(1)
            turned_out(1)
            maximum(3)
            normalise(2)
            if more:
                rotate(dve, h + 1, 1 - e)
            turned_out(2)
            normalise(3)
            turned_out(3)

        def head_pool(pool, i, e, load):
            h = 2 * i + e
            if load:
                split_head(pool, i + 1, e)
            at = slice(h, h + 1) if isinstance(h, int) else bass.ds(h, 1)
            pool.wait_ge(zt_ev, h + 1)
            pool.wait_ge(zh_ev, h + 1)
            nc.gpsimd.tensor_tensor(gate[:, at, :].bitcast(F32R), z_t[:].unsqueeze(1), z2_hi[:, at, :].bitcast(F32),
                                    ALU.subtract).then_inc(zl_ev, 1)
            pool.wait_ge(zl_ev, h + 1)

        with nc.Block() as block:
            @block.sync
            def _(sp):
                with sp.Fori(1, MH // 2) as i:
                    for e in range(2):
                        load_head(sp, 2 * i + e, e)
                for n in range(2):
                    load_unit(sp, U_MO + n, (U_MO + n) % 2, out_src(mla_out, 0, n))

            @block.gpsimd
            def _(pool):
                with pool.Fori(0, MH // 2 - 1) as i:
                    for e in range(2):
                        head_pool(pool, i, e, True)
                for e in range(2):
                    split_unit(pool, U_MO + e, (U_MO + e) % 2)
                    head_pool(pool, MH // 2 - 1, e, False)

            @block.tensor
            def _(pe):
                for n in range(4):
                    up_item(pe, 0, 0, n)
                all_heads(pe, head_pe)
                values(pe, MH - 1, 1)

            @block.scalar
            def _(act):
                for n in range(4):
                    up_out(act, 0, 0, n)
                all_heads(act, head_act)

            @block.vector
            def _(dve):
                rotate(dve, 0, 0)
                all_heads(dve, head_dve)
                gated(dve, MH - 1)

        put = region(ATTN_KB + 33)
        m2T = put("m2T", [P, KD, T1])
        o_tok = put("o_tok", [P, QB, D])
        norm_post1 = Norm(lambda j: m2T[:, j, :], KD, HALVES1, D, lambda j: prm("post", 8 + j), 6, 130)
        m2_out = sem("m2_out")
        res_done = sem("res_done")
        o_mm = sem("o_mm")
        o_ev = sem("o_ev")
        s_out = sem("s_out")

        with nc.Block() as block:
            @block.sync
            def _(sp):
                for n in (2, 3):
                    load_unit(sp, U_MO + n, (U_MO + n) % 2, out_src(mla_out, P, n - 2))
                with sp.Fori(1, 4) as j:
                    for e in range(2):
                        for half in range(2):
                            u = U_MO + 2 * e + half
                            load_unit(sp, 4 * j + u, u % 2, out_src(mla_out, 256 * j + P * e, half))
                for t in range(QB):
                    sp.wait_ge(o_ev, 2 * t + 2)
                    sp.dma_start(out[0, P * t:P * t + P, :], o_tok[:, t, :]).then_inc(s_out, 16)
                sp.wait_ge(s_out, 16 * QB)

            @block.gpsimd
            def _(pool):
                for n in (2, 3):
                    split_unit(pool, U_MO + n, (U_MO + n) % 2)
                with pool.Fori(1, 4) as j:
                    for n in range(4):
                        split_unit(pool, 4 * j + (U_MO + n), (U_MO + n) % 2)

            @block.tensor
            def _(pe):
                with pe.Fori(0, 4) as j:
                    for e in range(2):
                        out_products(pe, j, U_MO, e, lambda k, at, n: (z2_hi[:, k, at:at + n], gate[:, k, at:at + n].bitcast(F32R)),
                                     HALVES1, m2_out)
                norm_post1.pe(pe)
                for t in range(QB):
                    for half in range(2):
                        for k in range(4):
                            j = 4 * half + k
                            if t == 0:
                                pe.wait_ge(res_done, j + 1)
                            mm = nc.tensor.transpose(ps[:, 2 * t + half, P * k:P * k + P], m2T[:, j, P * t:P * t + P], ident[:])
                        mm.then_inc(o_mm, 1)

            @block.scalar
            def _(act):
                norm_post1.act(act, lambda e, j: e.wait_ge(m2_out, j + 2))

            @block.vector
            def _(dve):
                dve.sem_inc(m2_out, 1)
                with dve.Fori(0, 4) as j:
                    for e in range(2):
                        dve.wait_ge(unit_done, 4 * j + (U_MO + 2 * e + 2))
                        nc.vector.tensor_copy(m2T[:, bass.ds(2 * j + e, 1), :], ps[:, e:e + 1, :]).then_inc(m2_out, 1)
                dve.wait_ge(m2_out, KD + 1)
                norm_post1.dve(dve, y=lambda j: m2T[:, j, :])
                for j in range(KD):
                    nc.vector.tensor_tensor(m2T[:, j, :], m2T[:, j, :], xT[:, j, N_META:T2], ALU.add).then_inc(res_done, 1)
                for t in range(QB):
                    for half in range(2):
                        dve.wait_ge(o_mm, 2 * t + half + 1)
                        nc.vector.tensor_copy(o_tok[:, t, 512 * half:512 * half + 512], ps[:, 2 * t + half, :]).then_inc(o_ev, 1)


_INS = ["x", "norm_mix_g", "w_in", "b_f", "b_gate", "conv_mix_w", "w_out_conv", "w_out_attn", "w_o", "norm_ffn_g",
        "w_up", "conv_ffn_w", "w_down", "norm_f_g", "meta_tokens_2", "norm_pre_2", "norm_post_2", "rwkv_mu_2",
        "rwkv_w_in_2", "rwkv_w0_2", "rwkv_w2_2", "rwkv_a0_2", "rwkv_a2_2", "rwkv_k_k_2", "rwkv_k_a_2", "rwkv_r_k_2",
        "rwkv_ln_w_2", "rwkv_ln_b_2", "rwkv_w_out_2", "mla_w_in_2", "mla_q_norm_2", "mla_w_q_up_2", "mla_kv_norm_2",
        "mla_w_kv_up_2", "mla_w_out_2"]


def rope_tables():
    half = ROPE // 2
    inv = np.exp(-math.log(10000.0) * np.arange(half, dtype=np.float32) / half).astype(np.float32)
    ang = (inv[:, None] * np.arange(T2, dtype=np.float32)[None, :]).astype(np.float32)
    cos, sin = np.cos(ang), np.sin(ang)
    return np.concatenate([cos, cos]), np.concatenate([-sin, sin])


def kernel(**inputs):
    import concourse.bacc as _bacc
    from concourse.bass_utils import run_bass_kernel_spmd as _run

    nc = _bacc.Bacc("TRN2", target_bir_lowering=False, num_devices=1)
    arrays, io = {}, {}
    given = {name: np.ascontiguousarray(inputs[name]) for name in _INS}
    given["rope_cos"], given["rope_sin"] = rope_tables()
    for name, a in given.items():
        arrays[f"in_{name}_dram"] = a
        io[name] = nc.dram_tensor(f"in_{name}_dram", a.shape, mybir.dt.from_np(a.dtype), kind="ExternalInput").ap()
    out = nc.dram_tensor("out_0_dram", (1, T1, D), F32, kind="ExternalOutput").ap()
    program(nc, io, out)
    r = _run(nc, [arrays], core_ids=[0])
    return r.results[0]["out_0_dram"]
```
